# Optimizing a Trainium2 kernel written in Bass

```python
import math
import jax, jax.numpy as jnp
from jax import lax
import numpy as np

D_MODEL = 2048
BATCH = 1
SEQ = 256
DEPTH = 1
DEC_BATCH = 8
DEC_SEQ = 1
PAST_LEN = 1024
PAGE_SIZE = 128

N_HEADS = 8
HEAD_DIM = 64
V_DIM = 2 * HEAD_DIM
ATTN_QK = N_HEADS * 2 * HEAD_DIM
ATTN_WIDTH = N_HEADS * V_DIM
D_CONV = 1024
CONV_WIDTH = 3
D_FF = 5632
ROPE_THETA = 500000.0
ROT_DIM = HEAD_DIM // 4
Q_BLOCK = 128
LN_EPS = 1e-5
NEG_INF = -1e30
DEEPNORM_ALPHA = (2.0 * DEPTH) ** 0.25
DEEPNORM_BETA = (8.0 * DEPTH) ** -0.25
SPLIT_SIZES = (ATTN_QK, ATTN_QK, ATTN_WIDTH, D_CONV, D_CONV, D_CONV, D_MODEL, D_MODEL)
SPLIT_OFFSETS = [int(o) for o in np.cumsum(SPLIT_SIZES)[:-1]]
D_IN = int(sum(SPLIT_SIZES))

kernel_name = 'hybrid_diffattn_shortconv_macaron_deepnorm_step'

def layer_norm(x, g, b):
    xf = x.astype(jnp.float32)
    mu = jnp.mean(xf, axis=-1, keepdims=True)
    var = jnp.mean(jnp.square(xf - mu), axis=-1, keepdims=True)
    return ((xf - mu) * lax.rsqrt(var + LN_EPS)).astype(x.dtype) * g + b

def head_rmsnorm(o, g):
    of = o.astype(jnp.float32)
    return (of * lax.rsqrt(jnp.mean(of * of, axis=-1, keepdims=True) + LN_EPS)).astype(o.dtype) * g

def swiglu(x, w_gate, w_up, w_down):
    return (jax.nn.silu(x @ w_gate) * (x @ w_up)) @ w_down

def rope(x, pos):
    half = ROT_DIM // 2
    inv_freq = jnp.power(ROPE_THETA, -jnp.arange(0, ROT_DIM, 2, dtype=jnp.float32) / ROT_DIM)
    ang = pos.astype(jnp.float32)[:, None] * inv_freq[None, :]
    cos = jnp.cos(ang)[None, :, None, None, :].astype(x.dtype)
    sin = jnp.sin(ang)[None, :, None, None, :].astype(x.dtype)
    x1 = x[..., :half]
    x2 = x[..., half:ROT_DIM]
    return jnp.concatenate([x1 * cos - x2 * sin, x2 * cos + x1 * sin, x[..., ROT_DIM:]], axis=-1)

def diff_weights(s, lam):
    p = jax.nn.softmax(s, axis=-1)
    return p[:, :, 0] - lam * p[:, :, 1]

def prompt_attention(q, k, v, pos, lam):
    B, T = q.shape[0], q.shape[1]
    nb = T // Q_BLOCK
    scale = HEAD_DIM ** -0.5
    qb = q.reshape(B, nb, Q_BLOCK, N_HEADS, 2, HEAD_DIM).transpose(1, 0, 2, 3, 4, 5)
    pb = pos.reshape(nb, Q_BLOCK)

    def one_block(args):
        q_blk, p_blk = args
        s = jnp.einsum('bqhcd,bkhcd->bhcqk', q_blk, k).astype(jnp.float32) * scale
        mask = pos[None, :] <= p_blk[:, None]
        s = jnp.where(mask, s, NEG_INF)
        a = diff_weights(s, lam)
        return jnp.einsum('bhqk,bkhe->bqhe', a.astype(v.dtype), v)

    o = lax.map(one_block, (qb, pb))
    return o.transpose(1, 0, 2, 3, 4).reshape(B, T, N_HEADS, V_DIM)

def sample_attention(q, k_new, v_new, k_past, v_past, qpos, lam):
    P = k_past.shape[1]
    scale = HEAD_DIM ** -0.5
    s_past = jnp.einsum('bqhcd,bkhcd->bhcqk', q, k_past).astype(jnp.float32) * scale
    s_new = jnp.einsum('bqhcd,bkhcd->bhcqk', q, k_new).astype(jnp.float32) * scale
    s_new = jnp.where(qpos[None, :] <= qpos[:, None], s_new, NEG_INF)
    a = diff_weights(jnp.concatenate([s_past, s_new], axis=-1), lam).astype(v_new.dtype)
    return (jnp.einsum('bhqk,bkhe->bqhe', a[..., :P], v_past)
            + jnp.einsum('bhqk,bkhe->bqhe', a[..., P:], v_new))

def short_conv(u, buf, w):
    T = u.shape[1]
    up = jnp.concatenate([buf, u], axis=1)
    y = w[0] * up[:, 0:T] + w[1] * up[:, 1:T + 1] + w[2] * up[:, 2:T + 2]
    return y, up[:, T:]

def decoder_layer(x, pos, conv_buf, k_past, v_past, lambda_init, ln_g, ln_b,
                  ffn1_w_gate, ffn1_w_up, ffn1_w_down, w_in, conv_w,
                  lambda_q1, lambda_k1, lambda_q2, lambda_k2, subln_g,
                  w_attn_out, w_conv_out, w_o, ffn2_w_gate, ffn2_w_up, ffn2_w_down):
    B, T, _ = x.shape
    x = layer_norm(DEEPNORM_ALPHA * x + 0.5 * swiglu(x, ffn1_w_gate, ffn1_w_up, ffn1_w_down), ln_g[0], ln_b[0])
    z = x @ w_in
    q, k, v, c_b, c_c, c_h, g_attn, g_conv = jnp.split(z, SPLIT_OFFSETS, axis=-1)
    q = rope(q.reshape(B, T, N_HEADS, 2, HEAD_DIM), pos)
    k = rope(k.reshape(B, T, N_HEADS, 2, HEAD_DIM), pos)
    v = v.reshape(B, T, N_HEADS, V_DIM)
    lam = (jnp.exp(jnp.sum(lambda_q1.astype(jnp.float32) * lambda_k1.astype(jnp.float32)))
           - jnp.exp(jnp.sum(lambda_q2.astype(jnp.float32) * lambda_k2.astype(jnp.float32)))
           + lambda_init)
    if k_past is None:
        o = prompt_attention(q, k, v, pos, lam)
    else:
        o = sample_attention(q, k, v, k_past, v_past, pos, lam)
    o = head_rmsnorm(o, subln_g) * (1.0 - lambda_init)
    y_attn = o.reshape(B, T, ATTN_WIDTH) @ w_attn_out
    conv_out, new_buf = short_conv(c_c * c_h, conv_buf, conv_w)
    y_conv = (c_b * conv_out) @ w_conv_out
    merged = jax.nn.sigmoid(g_attn) * y_attn + jax.nn.sigmoid(g_conv) * y_conv
    x = layer_norm(DEEPNORM_ALPHA * x + merged @ w_o, ln_g[1], ln_b[1])
    x = layer_norm(DEEPNORM_ALPHA * x + 0.5 * swiglu(x, ffn2_w_gate, ffn2_w_up, ffn2_w_down), ln_g[2], ln_b[2])
    return x, k.reshape(B, T, N_HEADS, V_DIM), v, new_buf

def setup_inputs(seed: int = 0) -> dict:
    key = jax.random.key(seed)
    ks = jax.random.split(key, 24)
    n_pages = PAST_LEN // PAGE_SIZE
    n_used = DEC_BATCH * n_pages
    n_pool = n_used + (n_used + 3) // 4

    def nrm(k, shape, scale):
        return jax.random.normal(k, shape, jnp.float32) * scale

    return {
        'x_prompt': nrm(ks[0], (BATCH, SEQ, D_MODEL), 1.0),
        'x_sample': nrm(ks[1], (DEC_BATCH, DEC_SEQ, D_MODEL), 1.0),
        'cache_k': nrm(ks[2], (DEPTH, n_pool, PAGE_SIZE, N_HEADS, V_DIM), 1.0),
        'cache_v': nrm(ks[3], (DEPTH, n_pool, PAGE_SIZE, N_HEADS, V_DIM), 1.0),
        'state_conv': nrm(ks[4], (DEPTH, DEC_BATCH, CONV_WIDTH - 1, D_CONV), 1.0),
        'page_table': jax.random.permutation(ks[5], n_pool)[:n_used].reshape(DEC_BATCH, n_pages).astype(jnp.int32),
        'ln_g': 1.0 + nrm(ks[6], (DEPTH, 3, D_MODEL), 0.02),
        'ln_b': nrm(ks[7], (DEPTH, 3, D_MODEL), 0.02),
        'ffn1_w_gate': nrm(ks[8], (DEPTH, D_MODEL, D_FF), D_MODEL ** -0.5),
        'ffn1_w_up': nrm(ks[9], (DEPTH, D_MODEL, D_FF), D_MODEL ** -0.5),
        'ffn1_w_down': nrm(ks[10], (DEPTH, D_FF, D_MODEL), D_FF ** -0.5 * DEEPNORM_BETA),
        'w_in': nrm(ks[11], (DEPTH, D_MODEL, D_IN), D_MODEL ** -0.5),
        'conv_w': nrm(ks[12], (DEPTH, CONV_WIDTH, D_CONV), CONV_WIDTH ** -0.5),
        'lambda_q1': nrm(ks[13], (DEPTH, HEAD_DIM), 0.1),
        'lambda_k1': nrm(ks[14], (DEPTH, HEAD_DIM), 0.1),
        'lambda_q2': nrm(ks[15], (DEPTH, HEAD_DIM), 0.1),
        'lambda_k2': nrm(ks[16], (DEPTH, HEAD_DIM), 0.1),
        'subln_g': 1.0 + nrm(ks[17], (DEPTH, V_DIM), 0.02),
        'w_attn_out': nrm(ks[18], (DEPTH, ATTN_WIDTH, D_MODEL), ATTN_WIDTH ** -0.5 * DEEPNORM_BETA),
        'w_conv_out': nrm(ks[19], (DEPTH, D_CONV, D_MODEL), D_CONV ** -0.5 * DEEPNORM_BETA),
        'w_o': nrm(ks[20], (DEPTH, D_MODEL, D_MODEL), D_MODEL ** -0.5 * DEEPNORM_BETA),
        'ffn2_w_gate': nrm(ks[21], (DEPTH, D_MODEL, D_FF), D_MODEL ** -0.5),
        'ffn2_w_up': nrm(ks[22], (DEPTH, D_MODEL, D_FF), D_MODEL ** -0.5),
        'ffn2_w_down': nrm(ks[23], (DEPTH, D_FF, D_MODEL), D_FF ** -0.5 * DEEPNORM_BETA),
    }

def reference(x_prompt, x_sample, cache_k, cache_v, state_conv, page_table,
              ln_g, ln_b, ffn1_w_gate, ffn1_w_up, ffn1_w_down, w_in, conv_w,
              lambda_q1, lambda_k1, lambda_q2, lambda_k2, subln_g,
              w_attn_out, w_conv_out, w_o, ffn2_w_gate, ffn2_w_up, ffn2_w_down):
    B, T = x_prompt.shape[0], x_prompt.shape[1]
    DB, DT = x_sample.shape[0], x_sample.shape[1]
    past_len = page_table.shape[1] * PAGE_SIZE
    pos_p = jnp.arange(T, dtype=jnp.int32)
    pos_s = past_len + jnp.arange(DT, dtype=jnp.int32)
    y_p, y_s = x_prompt, x_sample
    kp_list, vp_list, cp_list, ks_list, vs_list, cs_list = [], [], [], [], [], []
    for layer in range(DEPTH):
        lambda_init = 0.8 - 0.6 * math.exp(-0.3 * layer)
        lp = (lambda_init, ln_g[layer], ln_b[layer], ffn1_w_gate[layer], ffn1_w_up[layer], ffn1_w_down[layer],
              w_in[layer], conv_w[layer], lambda_q1[layer], lambda_k1[layer], lambda_q2[layer], lambda_k2[layer],
              subln_g[layer], w_attn_out[layer], w_conv_out[layer], w_o[layer],
              ffn2_w_gate[layer], ffn2_w_up[layer], ffn2_w_down[layer])
        buf0 = jnp.zeros((B, CONV_WIDTH - 1, D_CONV), x_prompt.dtype)
        y_p, k_p, v_p, c_p = decoder_layer(y_p, pos_p, buf0, None, None, *lp)
        k_past = cache_k[layer, page_table].reshape(DB, past_len, N_HEADS, 2, HEAD_DIM)
        v_past = cache_v[layer, page_table].reshape(DB, past_len, N_HEADS, V_DIM)
        y_s, k_s, v_s, c_s = decoder_layer(y_s, pos_s, state_conv[layer], k_past, v_past, *lp)
        kp_list.append(k_p); vp_list.append(v_p); cp_list.append(c_p)
        ks_list.append(k_s); vs_list.append(v_s); cs_list.append(c_s)
    k_prompt = jnp.stack(kp_list)
    v_prompt = jnp.stack(vp_list)
    conv_prompt = jnp.stack(cp_list)
    k_sample = jnp.stack(ks_list)
    v_sample = jnp.stack(vs_list)
    conv_sample = jnp.stack(cs_list)
    return (y_prompt_out := y_p, y_s, k_prompt, v_prompt, conv_prompt, k_sample, v_sample, conv_sample)


_drawn_inputs = setup_inputs


def setup_inputs(seed=0):
    import zlib

    import numpy as np

    out = dict(_drawn_inputs(seed))
    spreads = {}
    factors = {'lambda_q1': 7.841, 'lambda_k1': 8.0, 'lambda_q2': 7.725, 'lambda_k2': 8.0, 'subln_g': 8.0}
    for name, (base, spread) in spreads.items():
        noise = np.random.default_rng([zlib.crc32(name.encode()), seed]).standard_normal(out[name].shape)
        drawn = base * np.exp(spread * noise) if base else spread * noise
        out[name] = __import__('jax').numpy.asarray(drawn.astype(out[name].dtype))
    for name, factor in factors.items():
        out[name] = (out[name] * factor).astype(out[name].dtype)
    return out
```

```python
from contextlib import ExitStack, contextmanager

import numpy as np
import concourse.bass as bass
from concourse import mybir

ALU = mybir.AluOpType
ACT = mybir.ActivationFunctionType
F32 = mybir.dt.float32
F32R = mybir.dt.float32r
I32 = mybir.dt.int32
AX = mybir.AxisListType.X

P = 128
D = 2048
T = 256
B = 8
N = T + B
F = 5632
HEADS, HD, VD = 8, 64, 128
DC = 1024
PAGE, PAGES = 128, 8
DT, FT, AT = D // P, F // P, DC // P
KC, MC = 4, 4
WC = MC * P
ALPHA = 2.0 ** 0.25
LN_EPS = 1e-5
LAMBDA_INIT = 0.8 - 0.6
SCALE = HD ** -0.5
NEG = -1e30
ROT = 8
SLOTS = PAGES + 1
PT = 2


class Count:

    def __init__(self, n=0):
        self.n, self.term = n, 0

    def __call__(self, ahead=0):
        return self.term + (self.n + ahead)

    def add(self, by=1):
        self.n += by
        return self()


@contextmanager
def loop(eng, times, *steps):
    with eng.Fori(0, times) as i:
        starts = [c.n for c, _ in steps]
        for c, s in steps:
            c.term = i * s
        yield i
        for (c, s), n in zip(steps, starts):
            assert c.n == n + s, (c.n, n, s)
    for (c, s), n in zip(steps, starts):
        c.term, c.n = 0, n + times * s


class Progress:

    def __init__(self):
        self.split = Count()
        self.landed = [Count(), Count()]
        self.tiles = Count()
        self.chunks = Count(2)
        self.out = [Count(MC), Count(MC)]

    def steps(self, chunks):
        return ((self.split, 2 * chunks), (self.landed[0], 16 * chunks), (self.landed[1], 16 * chunks),
                (self.tiles, 2 * (MC - 1)), (self.chunks, 2 * chunks), (self.out[0], MC), (self.out[1], MC))

    def skip_panel(self, banks, chunks):
        self.tiles.add(MC - 1)
        self.chunks.add(chunks)
        self.out[banks].add(MC)


def program(nc, a, out):
    with ExitStack() as ctx:
        def sem(name):
            return ctx.enter_context(nc.semaphore(name))

        top = nc.sbuf_base
        end = nc.sbuf_usable_end

        def at(name, shape, dt=F32, offset=None):
            nonlocal top
            size = int(np.prod(shape[1:])) * 4
            if offset is None:
                top = -(-top // 32) * 32
                offset, top = top, top + size
            assert offset + size <= end, (name, offset, size, end)
            return nc.alloc_sbuf_tensor_at(name, shape, dt, offset=offset)

        TILE = N * 4
        x_at = (top + 31) // 32 * 32
        x_hi = at("x_hi", [P, DT, N], F32R)
        x_lo = at("x_lo", [P, DT, N], F32R)
        y = at("y", [P, DT, N], F32, x_at)
        y_norm = at("y_norm", [P, DT, N], F32, x_at + DT * TILE)
        w_raw = at("w_raw", [P, 2, KC, WC])
        w_hi = at("w_hi", [P, 2, KC, WC], F32R)
        w_lo = at("w_lo", [P, 2, KC, WC], F32R)
        ident = at("ident", [P, P])
        ones = at("ones", [P, P])
        mask = at("mask", [P, 3, P])
        ln_g = at("ln_g", [P, 3, DT])
        ln_b = at("ln_b", [P, 3, DT])
        conv_w = at("conv_w", [P, 3, AT])
        conv_state = at("conv_state", [P, AT, B, 2])
        rope_cs = at("rope_cs", [P, 2, 3, ROT])
        subln = at("subln", [P, 1])
        lam_in = at("lam_in", [HD, 4])
        lam_prod = at("lam_prod", [HD, 2])
        lam = at("lam", [P, 4])
        page_ids = at("page_ids", [1, B * PAGES], I32)
        neg_eye = at("neg_eye", [B, B])
        one_sum = at("one_sum", [P, N])
        mean = at("mean", [P, N])
        rstd = at("rstd", [P, N])
        eps = at("eps", [P, 2])
        area = (top + 31) // 32 * 32

        h_hi = at("h_hi", [P, FT, N], F32R, area)
        h_lo = at("h_lo", [P, FT, N], F32R, area + FT * TILE)
        hid = at("hid", [P, MC, N], F32, area + 2 * FT * TILE)

        top = area
        o_all = at("o_all", [P, HEADS, N])
        scores = at("scores", [P, B, SLOTS, 2 * HEADS])
        k_ring = at("k_ring", [P, 2, DC])
        qb_at = (top + 31) // 32 * 32
        q_bcast = at("q_bcast", [P, B, DC])
        v_ring = at("v_ring", [P, 8, DC], F32, qb_at)
        m_hi = at("m_hi", [P, DT, N], F32R, qb_at)
        m_lo = at("m_lo", [P, DT, N], F32R, qb_at + DT * TILE)
        v_s = at("v_s", [B, DC])
        assert 2 * DT * TILE <= (B + 1) * DC * 4
        early = (top + 31) // 32 * 32
        z_q = at("z_q", [P, AT, N])
        z_k = at("z_k", [P, AT, N])
        zv_at = (top + 31) // 32 * 32
        z_v = at("z_v", [P, AT, N])
        qk_tok = at("qk_tok", [P, 3, DC])
        v_tok = at("v_tok", [P, PT, DC])
        q_s = at("q_s", [B, DC])
        rope_at = (top + 31) // 32 * 32
        rope_t = at("rope_t", [P, 4, PT, 2 * HEADS, ROT])
        stats = at("stats", [P, 2, 16])
        s_tmp = at("s_tmp", [B, 2, 2 * HEADS])
        prob = at("prob", [P, 2, 2, 3, P], F32, zv_at)
        attn = at("attn", [P, 3, P], F32, zv_at + 6144)
        attn_t = at("attn_t", [P, 3, P], F32, rope_at)
        top = early
        c_at = early
        z_c = at("z_c", [P, 3, AT, N])
        sig = at("sig", [P, 2, DT, N])
        sig_at = early + 3 * AT * TILE
        u_pad = at("u_pad", [P, AT, 2 + T], F32, sig_at)
        u_s = at("u_s", [P, AT, B], F32, sig_at + 9216)
        conv_o = at("conv_o", [P, AT, N], F32, sig_at + 10240)
        conv_t = at("conv_t", [P, 3, AT, B], F32, sig_at + 19456)
        conv_new = at("conv_new", [P, AT, B, 2], F32, sig_at + 20480)
        yc_hi = at("yc_hi", [P, AT, N], F32R, c_at + AT * TILE)
        yc_lo = at("yc_lo", [P, AT, N], F32R, c_at + 2 * AT * TILE)
        o_hi = at("o_hi", [P, AT, N], F32R, c_at)
        o_lo = at("o_lo", [P, AT, N], F32R, c_at + AT * TILE)
        o_sq = at("o_sq", [P, AT, N], F32, c_at + 2 * AT * TILE)
        kr_at = qb_at - 2 * DC * 4
        s_max = at("s_max", [P, P], F32, kr_at)
        s_diag = at("s_diag", [P, P], F32, kr_at + 512)
        s_rec = at("s_rec", [P, P], F32, kr_at + 1024)
        s_attn = at("s_attn", [P, B, SLOTS, HEADS], F32, kr_at + 1536)
        s_attn2 = at("s_attn2", [P, B, SLOTS, HEADS], F32, kr_at + 4096)
        s_col = at("s_col", [P, 1], F32, kr_at + 7168)

        ps = ctx.enter_context(nc.psum_tensor("ps", [P, 8, 512], F32))

        const_in = sem("const_in")
        page_ids_in = sem("page_ids_in")
        x_in = sem("x_in")
        made = sem("made")
        w_landed = [sem("w_landed0"), sem("w_landed1")]
        w_hi_ready = sem("w_hi_ready")
        w_lo_ready = sem("w_lo_ready")
        w_used = sem("w_used")
        tile_done = sem("tile_done")
        out_of = [sem("out_of_banks0"), sem("out_of_banks1")]
        x_hi_ready = sem("x_hi_ready")
        x_ready = sem("x_ready")
        h_hi_ready = sem("h_hi_ready")
        h_ready = sem("h_ready")
        dve_step = sem("dve_step")
        lam_prod_ready = sem("lam_prod_ready")
        lam_sum = sem("lam_sum")
        lam_exp = sem("lam_exp")
        ln_partial = sem("ln_partial")
        ln_summed = sem("ln_summed")
        ln_centered = sem("ln_centered")
        ln_squared = sem("ln_squared")
        ln_squares = sem("ln_squares")
        ln_var = sem("ln_var")
        ln_std = sem("ln_std")
        ln_out = sem("ln_out")
        turned = sem("turned")
        tok_ready = sem("tok_ready")
        roped = sem("roped")
        q_kept = sem("q_kept")
        back = sem("back")
        back_ready = sem("back_ready")
        q_stored = sem("q_stored")
        qb_landed = sem("qb_landed")
        k_landed = [sem("k_landed0"), sem("k_landed1")]
        k_free = sem("k_free")
        v_landed = [sem(f"v_landed{i}") for i in range(PAGES)]
        v_used = sem("v_used")
        sc_done = sem("sc_done")
        sc_masked = sem("sc_masked")
        sc_max = sem("sc_max")
        sc_exp = sem("sc_exp")
        at_ready = sem("at_ready")
        at_turned = sem("at_turned")
        att_ready = sem("att_ready")
        pv_done = sem("pv_done")
        o_ready = sem("o_ready")
        conv_done = sem("conv_done")
        conv_new_ready = sem("conv_new_ready")
        conv_hi = sem("conv_hi")
        yc_ready = sem("yc_ready")
        ss_max1 = sem("ss_max1")
        ss_turned = sem("ss_turned")
        ss_diag = sem("ss_diag")
        ss_bcast = sem("ss_bcast")
        ss_shift = sem("ss_shift")
        ss_exp = sem("ss_exp")
        ss_sums = sem("ss_sums")
        ss_den = sem("ss_den")
        ss_attn = sem("ss_attn")
        o_s_ready = sem("o_s_ready")
        o_square = sem("o_square")
        o_sumsq = sem("o_sumsq")
        o_std = sem("o_std")
        o_scaled = sem("o_scaled")
        o_hi_ready = sem("o_hi_ready")
        o_split = sem("o_split")
        m_sum = sem("m_sum")
        m_hi_ready = sem("m_hi_ready")
        m_ready = sem("m_ready")
        kv_stored = sem("kv_stored")
        conv_stored = sem("conv_stored")
        y_stored = sem("y_stored")

        q_scratch = nc.dram_tensor("q_scratch", [B, DC], F32, kind="Internal").ap()
        block = ctx.enter_context(nc.Block())

        K_CH, H_CH, A_CH = DT // KC, FT // KC, AT // KC
        FFN_PAIRS = F // WC
        OUT_PAIRS = D // WC // 2
        C_PAIRS = 3 * DC // (2 * WC)
        G_PAIRS = 2 * D // (2 * WC)
        CONSTS, MADE = 16 * 7, 8

        @block.sync
        def _(sp):
            n = Count()
            pages = Count()

            def chunk(w, k0, col):
                sp.wait_ge(w_lo_ready, n.add())
                s = (n.n - 1) % 2
                src = w[k0 * P:(k0 + KC) * P, bass.ds(col, WC)].rearrange("(k p) n -> p k n", p=P)
                sp.dma_start(w_raw[:, s], src).then_inc(w_landed[s], 16)

            def ffn(gate, up, down):
                with loop(sp, FFN_PAIRS, (n, 2 * K_CH)) as i:
                    for w in (gate, up):
                        for c in range(K_CH):
                            chunk(w, KC * c, i * WC)
                out_proj(down, H_CH)

            def out_pair(w, chunks, i, part=slice(None)):
                for p, c in [(p, c) for p in range(2) for c in range(chunks)][part]:
                    chunk(w, KC * c, i * (2 * WC) + p * WC)

            def out_proj(w, chunks):
                with loop(sp, OUT_PAIRS, (n, 2 * chunks)) as i:
                    out_pair(w, chunks, i)

            def page(cache, t, dst):
                p = sp.value_load(page_ids[0:1, bass.ds(t, 1)], min_val=0, max_val=cache.shape[1] - 1)
                return sp.dma_start(dst, cache[0, bass.ds(p, 1)].rearrange("a k h e -> (a k) (h e)"))

            def w_in_pair(i, seq=None):
                for p in range(2):
                    for c in range(K_CH):
                        chunk(a["w_in"][0], KC * c, i * (2 * WC) + p * WC)
                        if seq is not None:
                            j = p * K_CH + c
                            sp.wait_ge(k_free, pages.add())
                            page(a["cache_k"], seq * PAGES + j, k_ring[:, j % 2]).then_inc(k_landed[j % 2], 16)

            sp.dma_start(y_norm[:, :, 0:T], a["x_prompt_t"].rearrange("(t p) n -> p t n", p=P)).then_inc(x_in, 16)
            sp.dma_start(y_norm[:, :, T:N], a["x_sample_t"].rearrange("(t p) n -> p t n", p=P)).then_inc(x_in, 16)
            sp.dma_start(page_ids[:], a["page_table"]).then_inc(page_ids_in, 16)
            ffn(a["ffn1_w_gate"][0], a["ffn1_w_up"][0], a["ffn1_w_down"][0])
            w_in_pair(0)
            sp.wait_ge(page_ids_in, 16)
            w_in_pair(1)
            sp.wait_ge(q_kept, 1)
            sp.dma_start(q_scratch, q_s[:]).then_inc(q_stored, 16)
            sp.wait_ge(q_stored, 16)
            for b in range(B):
                sp.dma_start(q_bcast[:, b], q_scratch[b:b + 1].broadcast_to([P, DC])).then_inc(qb_landed, 16)
            with loop(sp, B, (n, 2 * K_CH), (pages, PAGES)) as i:
                w_in_pair(i + 2, i)

            def v_pages(b):
                for j in range(PAGES):
                    sp.wait_ge(v_used, b * PAGES + (j + 1))
                    page(a["cache_v"], b * PAGES + j, v_ring[:, j]).then_inc(v_landed[j], 16)

            out_pair(a["w_conv_out"][0], A_CH, 0)
            sp.wait_ge(k_free, 2 + B * PAGES)
            v_pages(0)
            out_pair(a["w_conv_out"][0], A_CH, 1)
            out_pair(a["w_attn_out"][0], A_CH, 0, slice(0, 2))
            with loop(sp, B - 1) as i:
                v_pages(i + 1)
            out_pair(a["w_attn_out"][0], A_CH, 0, slice(2, None))
            out_pair(a["w_attn_out"][0], A_CH, 1)
            out_proj(a["w_o"][0], K_CH)
            ffn(a["ffn2_w_gate"][0], a["ffn2_w_up"][0], a["ffn2_w_down"][0])
            sp.wait_ge(ln_out, 3)
            sp.dma_start(out["y_t"].rearrange("(t p) n -> p t n", p=P), y_norm[:]).then_inc(y_stored, 16)
            sp.wait_ge(y_stored, 16)
            sp.wait_ge(kv_stored, 16 * 4)
            sp.wait_ge(conv_stored, 16 * 2)

        @block.gpsimd
        def _(pool):
            nc.gpsimd.memset(ones[:], 1.0).then_inc(made, 1)
            nc.gpsimd.memset(ident[:], 0.0).then_inc(made, 1)
            nc.gpsimd.memset(mask[:], 0.0).then_inc(made, 1)
            nc.gpsimd.memset(eps[:, 0:1], LN_EPS / ALPHA ** 2).then_inc(made, 1)
            nc.gpsimd.memset(eps[:, 1:2], LN_EPS).then_inc(made, 1)
            pool.wait_ge(made, 5)
            nc.gpsimd.affine_select(out=ident[:], in_=ident[:], compare_op=ALU.not_equal, fill=1.0, base=0,
                                    pattern=[[-1, P]], channel_multiplier=1).then_inc(made, 1)
            for j in (0, 2):
                nc.gpsimd.affine_select(out=mask[:, j], in_=mask[:, j], compare_op=ALU.is_ge, fill=NEG, base=0,
                                        pattern=[[-1, P]], channel_multiplier=1).then_inc(made, 1)
            for dst, src in ((ln_g, "ln_g"), (ln_b, "ln_b"), (conv_w, "conv_w"), (conv_state, "state_conv"),
                             (rope_cs, "rope"), (subln, "subln_g"), (lam_in, "lambdas")):
                pool.dma_start(dst[:], a[src]).then_inc(const_in, 16)

        @block.tensor
        def _(pe):
            n = Count()
            uses = [Count(), Count()]

            def panel(banks, hi, lo, chunks):
                for c in range(chunks):
                    pe.wait_ge(w_lo_ready, n.add() + 2)
                    s = (n.n - 1) % 2
                    for m in range(MC):
                        acc = ps[:, 4 * banks + m, 0:N]
                        if c == 0:
                            pe.wait_ge(out_of[banks], uses[banks].add())
                        for k in range(KC):
                            kt = c * KC + k
                            wh, wl = w_hi[:, s, k, m * P:(m + 1) * P], w_lo[:, s, k, m * P:(m + 1) * P]
                            nc.tensor.matmul(acc, wh, hi[:, kt], start=(kt == 0), stop=False)
                            nc.tensor.matmul(acc, wh, lo[:, kt], start=False, stop=False)
                            mm = nc.tensor.matmul(acc, wl, hi[:, kt], start=False, stop=(kt == chunks * KC - 1))
                        if m == MC - 1:
                            mm.then_inc(w_used, 1)
                        elif c == chunks - 1:
                            mm.then_inc(tile_done, 1)

            def pairs(times, hi, lo, chunks):
                with loop(pe, times, (n, 2 * chunks), (uses[0], MC), (uses[1], MC)):
                    for banks in range(2):
                        panel(banks, hi, lo, chunks)

            def pair(hi, lo, chunks):
                for banks in range(2):
                    panel(banks, hi, lo, chunks)

            def ffn(k):
                pairs(FFN_PAIRS, x_hi, x_lo, K_CH)
                pe.wait_ge(h_ready, 1 + FFN_PAIRS * k)
                pairs(OUT_PAIRS, h_hi, h_lo, H_CH)

            def banks_free():
                for banks in range(2):
                    pe.wait_ge(out_of[banks], uses[banks](MC))

            def layer_norm(k):
                banks_free()
                pe.wait_ge(ln_partial, k)
                nc.tensor.matmul(ps[:, 0, 0:N], ones[:], one_sum[:], start=True, stop=True).then_inc(ln_summed, 1)
                pe.wait_ge(ln_squares, k)
                nc.tensor.matmul(ps[:, 1, 0:N], ones[:], one_sum[:], start=True, stop=True).then_inc(ln_var, 1)

            def to_tokens(z):
                for j in range(3):
                    for t in range(AT):
                        w = P if j < PT else B
                        mm = nc.tensor.transpose(ps[0:w, 2 * j + t // 4, (t % 4) * P:(t % 4 + 1) * P],
                                                 z[:, t, j * P:j * P + w], ident[:])
                mm.then_inc(turned, 1)

            def from_tokens():
                for h in range(HEADS):
                    for j in range(PT):
                        mm = nc.tensor.transpose(ps[:, h // 2, (h % 2) * T + j * P:(h % 2) * T + (j + 1) * P],
                                                 qk_tok[:, j, h * VD:(h + 1) * VD], ident[:])
                mm.then_inc(back, 1)

            pe.sem_inc(w_used, 2)
            pe.sem_inc(v_used, PAGES)
            for banks in range(2):
                pe.sem_inc(out_of[banks], MC)
            pe.wait_ge(made, MADE)
            pe.wait_ge(lam_prod_ready, 2)
            nc.tensor.matmul(ps[:, 7, 0:2], ones[0:HD, :], lam_prod[:], start=True, stop=True).then_inc(lam_sum, 1)
            pe.wait_ge(lam_exp, 1)
            pe.wait_ge(x_ready, 1)
            ffn(1)
            layer_norm(1)
            pe.wait_ge(x_ready, 2)
            pair(x_hi, x_lo, K_CH)
            banks_free()
            to_tokens(z_q)
            pe.wait_ge(roped, 1)
            from_tokens()
            pe.wait_ge(back_ready, 1)
            pairs(2, x_hi, x_lo, K_CH)
            banks_free()
            to_tokens(z_k)
            pe.wait_ge(tok_ready, 6)
            pe.wait_ge(roped, 2)
            from_tokens()
            pe.wait_ge(back_ready, 2)
            to_tokens(z_v)
            pe.wait_ge(tok_ready, 9)

            def prompt_scores(h):
                if h >= 2:
                    pe.wait_ge(sc_masked, 2 * (h - 1))
                for c in range(2):
                    q, k = z_q[c * HD:(c + 1) * HD, h], z_k[c * HD:(c + 1) * HD, h]
                    bank = 2 * (h % 2) + c
                    nc.tensor.matmul(ps[:, bank, 0:P], q[:, 0:P], k[:, 0:P], start=True, stop=True)
                    mm = nc.tensor.matmul(ps[:, bank, P:3 * P], q[:, P:T], k[:, 0:T], start=True, stop=True)
                mm.then_inc(sc_done, 1)

            def prompt_values(h):
                pe.wait_ge(at_ready, h + 1)
                if h >= 1:
                    pe.wait_ge(att_ready, h)
                for b in range(3):
                    mm = nc.tensor.transpose(ps[:, 4, b * P:(b + 1) * P], attn[:, b], ident[:])
                mm.then_inc(at_turned, 1)
                pe.wait_ge(att_ready, h + 1)
                if h >= 1:
                    pe.wait_ge(o_ready, h)
                v = v_tok[:, :, h * VD:(h + 1) * VD]
                nc.tensor.matmul(ps[:, 5, 0:P], v[:, 0], attn_t[:, 0], start=True, stop=True)
                nc.tensor.matmul(ps[:, 5, P:T], v[:, 0], attn_t[:, 1], start=True, stop=False)
                nc.tensor.matmul(ps[:, 5, P:T], v[:, 1], attn_t[:, 2], start=False, stop=True).then_inc(pv_done, 1)

            prompt_scores(0)
            prompt_scores(1)
            for h in range(HEADS):
                prompt_values(h)
                if h + 2 < HEADS:
                    prompt_scores(h + 2)
            pe.wait_ge(o_ready, HEADS)
            pairs(C_PAIRS, x_hi, x_lo, K_CH)
            pairs(G_PAIRS, x_hi, x_lo, K_CH)
            pe.wait_ge(yc_ready, 1)
            pairs(OUT_PAIRS, yc_hi, yc_lo, A_CH)
            banks_free()
            pe.wait_ge(ss_max1, 1)
            nc.tensor.transpose(ps[:, 0, 0:P], s_max[:], ident[:]).then_inc(ss_turned, 1)
            pe.wait_ge(ss_diag, 1)
            nc.tensor.matmul(ps[:, 1, 0:P], ones[:], s_diag[:], start=True, stop=True).then_inc(ss_bcast, 1)
            pe.wait_ge(ss_sums, 1)
            nc.tensor.matmul(ps[:, 2, 0:P], ones[:], s_max[:], start=True, stop=True).then_inc(ss_den, 1)
            pe.wait_ge(ss_attn, 1)
            o_new = ps[:, 3, 0:B * HEADS].rearrange("p (b h) -> p b h", b=B)
            for h in range(HEADS):
                nc.tensor.matmul(o_new[:, :, h], v_s[:, h * VD:(h + 1) * VD], s_attn[0:B, :, PAGES, h],
                                 start=(h == 0), stop=True, skip_group_check=True)
            weights = s_attn[:].rearrange("p b s h -> p (b s h)")
            with loop(pe, B) as b:
                for j in range(PAGES):
                    pe.wait_ge(v_landed[j], b * 16 + 16)
                    for h in range(HEADS):
                        mm = nc.tensor.matmul(ps[:, 3, bass.ds(b * HEADS + h, 1)], v_ring[:, j, h * VD:(h + 1) * VD],
                                              weights[:, bass.ds(b * (SLOTS * HEADS) + j * HEADS + h, 1)],
                                              start=False, stop=True, skip_group_check=True)
                    mm.then_inc(v_used, 1)
            pe.wait_ge(o_square, 1)
            sq = o_sq[:].rearrange("p h n -> p (h n)")
            for c in range(5):
                w = min(512, AT * N - 512 * c)
                bank = (c + 4) % 8
                mm = nc.tensor.matmul(ps[:, bank, 0:w], ones[:], sq[:, c * 512:c * 512 + w], start=True, stop=True)
            mm.then_inc(o_sumsq, 1)
            pe.wait_ge(o_split, 1)
            pairs(OUT_PAIRS, o_hi, o_lo, A_CH)
            pe.wait_ge(m_ready, OUT_PAIRS)
            pairs(OUT_PAIRS, m_hi, m_lo, K_CH)
            layer_norm(2)
            pe.wait_ge(x_ready, 3)
            ffn(2)
            layer_norm(3)

        @block.scalar
        def _(sc):
            at_ = Progress()
            n, out_n = at_.split, at_.out
            panels_h = Count()

            def split_hi(times):
                for _ in range(times):
                    s = n.n % 2
                    sc.wait_ge(w_used, n(1))
                    sc.wait_ge(w_landed[s], at_.landed[s].add(16))
                    n.add()
                    nc.scalar.activation(w_hi[:, s], w_raw[:, s], ACT.Copy).then_inc(w_hi_ready, 1)

            def take_out(banks, chunks, func, dst):
                at_.chunks.add(chunks)
                for m in range(MC):
                    if m < MC - 1:
                        sc.wait_ge(tile_done, at_.tiles.add())
                    else:
                        sc.wait_ge(w_used, at_.chunks())
                    nc.scalar.activation(dst(m), ps[:, 4 * banks + m, 0:N], func).then_inc(out_of[banks], 1)
                    out_n[banks].add()

            def ffn(last=False):
                with loop(sc, FFN_PAIRS, *at_.steps(K_CH), (panels_h, 1)) as i:
                    split_hi(K_CH)
                    sc.wait_ge(h_ready, panels_h(1))
                    take_out(0, K_CH, ACT.Silu, lambda m: hid[:, m])
                    split_hi(K_CH)
                    at_.skip_panel(1, K_CH)
                    sc.wait_ge(out_of[1], out_n[1]())
                    nc.scalar.activation(h_hi[:, bass.ds(i * MC, MC)], hid[:], ACT.Copy).then_inc(h_hi_ready, 1)
                    panels_h.add()
                if last:
                    split_hi(2 * H_CH * OUT_PAIRS - 1)
                else:
                    only_split(OUT_PAIRS, H_CH)

            def only_split(times, chunks):
                with loop(sc, times, *at_.steps(chunks)):
                    split_hi(2 * chunks)
                    at_.skip_panel(0, chunks)
                    at_.skip_panel(1, chunks)

            def layer_norm(k):
                sc.wait_ge(ln_centered, k)
                nc.scalar.activation(y_norm[:], y[:], ACT.Square).then_inc(ln_squared, 1)
                sc.wait_ge(ln_var, k)
                nc.scalar.activation(rstd[:], ps[:, 1, 0:N], ACT.Sqrt, bias=eps[:, 0:1], scale=1.0 / D).then_inc(ln_std, 1)
                if k < 3:
                    sc.wait_ge(ln_out, k)
                    nc.scalar.activation(x_hi[:], y_norm[:], ACT.Copy).then_inc(x_hi_ready, 1)

            def z_pair(tile, func=ACT.Copy):
                for banks in range(2):
                    split_hi(K_CH)
                    take_out(banks, K_CH, func, lambda m: tile(MC * banks + m))

            def tokens(*dst):
                k = tokens.n = tokens.n + 1
                sc.wait_ge(turned, k)
                for j, d in enumerate(dst):
                    w = P if j < PT else B
                    src = ps[0:w, 2 * j:2 * j + 2].rearrange("p b n -> p (b n)")
                    nc.scalar.activation(d, src, ACT.Copy).then_inc(tok_ready, 1)
            tokens.n = 0

            def turned_back(k, z):
                sc.wait_ge(back, k)
                nc.scalar.activation(z[:, :, 0:T], ps[:, 0:4].rearrange("p b (h t) -> p (b h) t", h=2),
                                     ACT.Copy).then_inc(back_ready, 1)

            sc.wait_ge(x_in, 32)
            nc.scalar.activation(x_hi[:], y_norm[:], ACT.Copy).then_inc(x_hi_ready, 1)
            sc.wait_ge(lam_sum, 1)
            nc.scalar.activation(lam[:, 0:2], ps[:, 7, 0:2], ACT.Exp).then_inc(lam_exp, 1)
            split_hi(1)
            ffn()
            layer_norm(1)
            z_pair(lambda m: z_q[:, m])
            tokens(qk_tok[:, 0], qk_tok[:, 1], qk_tok[0:B, 2])
            turned_back(1, z_q)
            z_pair(lambda m: z_k[:, m])
            z_pair(lambda m: z_v[:, m])
            sc.wait_ge(q_kept, 1)
            tokens(qk_tok[:, 0], qk_tok[:, 1], qk_tok[0:B, 2])
            turned_back(2, z_k)
            tokens(v_tok[:, 0], v_tok[:, 1], v_s[:])
            sc.wait_ge(tok_ready, 9)
            for dst, src in (("k_prompt", qk_tok[:, 0:PT]), ("v_prompt", v_tok[:])):
                sc.dma_start(out[dst].rearrange("(j p) e -> p j e", p=P), src).then_inc(kv_stored, 16)
            for dst, src in (("k_sample", qk_tok[0:B, 2]), ("v_sample", v_s[:])):
                sc.dma_start(out[dst], src).then_inc(kv_stored, 16)

            def prompt_exp(h):
                sc.wait_ge(sc_max, h + 1)
                s = h % 2
                for c in range(2):
                    for j in range(2):
                        blocks = prob[:, s, c, 0:1] if j == 0 else prob[:, s, c, 1:3]
                        i = 2 * c + j
                        nc.scalar.activation(blocks, blocks, ACT.Exp, bias=stats[:, s, 4 + i:5 + i],
                                             accum_out=stats[:, s, 8 + i:9 + i]).then_inc(sc_exp, 1)

            def prompt_out(h):
                sc.wait_ge(at_turned, h + 1)
                if h >= 1:
                    sc.wait_ge(pv_done, h)
                nc.scalar.activation(attn_t[:], ps[:, 4, 0:3 * P].rearrange("p (b q) -> p b q", b=3),
                                     ACT.Copy).then_inc(att_ready, 1)
                sc.wait_ge(pv_done, h + 1)
                nc.scalar.activation(o_all[:, h, 0:T], ps[:, 5, 0:T], ACT.Copy).then_inc(o_ready, 1)

            for h in range(HEADS):
                prompt_exp(h)
                if h >= 1:
                    prompt_out(h - 1)
            prompt_out(HEADS - 1)

            z_all = z_c[:].rearrange("p c t n -> p (c t) n")
            sig_all = sig[:].rearrange("p c t n -> p (c t) n")
            sc.wait_ge(kv_stored, 16 * 4)
            sc.wait_ge(sc_masked, 2 * HEADS)
            with loop(sc, C_PAIRS, *at_.steps(K_CH)) as i:
                z_pair(lambda m: z_all[:, bass.ds(i * 8 + m, 1)])
            sc.wait_ge(conv_new_ready, 2)
            sc.dma_start(out["conv_prompt_t"].rearrange("(t p) k -> p t k", p=P), u_pad[:, :, T:T + 2]).then_inc(conv_stored, 16)
            sc.dma_start(out["conv_sample_t"].rearrange("(t p) b k -> p t b k", p=P), conv_new[:]).then_inc(conv_stored, 16)
            sc.wait_ge(conv_done, 1)
            nc.scalar.activation(yc_hi[:], conv_o[:], ACT.Copy).then_inc(conv_hi, 1)
            sc.wait_ge(yc_ready, 1)
            sc.wait_ge(conv_stored, 16 * 2)
            with loop(sc, G_PAIRS, *at_.steps(K_CH)) as i:
                z_pair(lambda m: sig_all[:, bass.ds(i * 8 + m, 1)], ACT.Sigmoid)
            only_split(OUT_PAIRS, A_CH)
            sc.wait_ge(ss_shift, 1)
            nc.scalar.activation(scores[:], scores[:], ACT.Exp, scale=SCALE).then_inc(ss_exp, 1)
            sc.wait_ge(v_used, PAGES + B * PAGES)
            nc.scalar.activation(o_all[:, :, T:N].rearrange("p h b -> p b h"),
                                 ps[:, 3, 0:B * HEADS].rearrange("p (b h) -> p b h", b=B), ACT.Copy).then_inc(o_s_ready, 1)
            sc.wait_ge(o_s_ready, 1)
            nc.scalar.activation(o_sq[:], o_all[:], ACT.Square).then_inc(o_square, 1)
            sc.wait_ge(o_sumsq, 1)
            sq = o_sq[:].rearrange("p h n -> p (h n)")
            nc.scalar.activation(sq[:, 0:2048], ps[:, 4:8].rearrange("p b n -> p (b n)"), ACT.Sqrt,
                                 bias=eps[:, 1:2], scale=1.0 / VD).then_inc(o_std, 1)
            nc.scalar.activation(sq[:, 2048:], ps[:, 0, 0:AT * N - 2048], ACT.Sqrt,
                                 bias=eps[:, 1:2], scale=1.0 / VD).then_inc(o_std, 1)
            sc.wait_ge(o_scaled, 1)
            nc.scalar.activation(o_hi[:], o_all[:], ACT.Copy).then_inc(o_hi_ready, 1)
            panels_m = Count()
            with loop(sc, OUT_PAIRS, *at_.steps(A_CH), (panels_m, 2)) as i:
                split_hi(2 * A_CH)
                at_.skip_panel(0, A_CH)
                at_.skip_panel(1, A_CH)
                sc.wait_ge(m_sum, panels_m.add(2))
                nc.scalar.activation(m_hi[:, bass.ds(i * 8, 8)], sig[:, 1, bass.ds(i * 8, 8)], ACT.Copy).then_inc(m_hi_ready, 1)
            only_split(OUT_PAIRS, K_CH)
            layer_norm(2)
            ffn(last=True)
            layer_norm(3)

        @block.vector
        def _(v):
            at_ = Progress()
            n, out_n = at_.split, at_.out
            own = Count()
            panels_h = Count()
            V = nc.vector

            def then(ins):
                ins.then_inc(dve_step, 1)
                v.wait_ge(dve_step, own.add())

            def split_lo(times, page=None):
                for c in range(times):
                    s = n.n % 2
                    v.wait_ge(w_hi_ready, n.add())
                    at_.landed[s].add(16)
                    V.tensor_tensor(w_lo[:, s], w_raw[:, s], w_hi[:, s].bitcast(F32), ALU.subtract).then_inc(w_lo_ready, 1)
                    if page is not None:
                        page(c)

            def wait_tile(m, chunks):
                if m == 0:
                    at_.chunks.add(chunks)
                if m < MC - 1:
                    v.wait_ge(tile_done, at_.tiles.add())
                else:
                    v.wait_ge(w_used, at_.chunks())

            def residual_panel(banks, chunks, t0, factor):
                part = y[:, bass.ds(t0, MC)]
                then(V.tensor_tensor(part, x_hi[:, bass.ds(t0, MC)].bitcast(F32),
                                     x_lo[:, bass.ds(t0, MC)].bitcast(F32), ALU.add))
                for m in range(MC):
                    wait_tile(m, chunks)
                    tile = y[:, bass.ds(t0 + m, 1)].rearrange("p a n -> p (a n)")
                    V.scalar_tensor_tensor(tile, ps[:, 4 * banks + m, 0:N], factor, tile,
                                           ALU.mult, ALU.add).then_inc(out_of[banks], 1)
                    out_n[banks].add()

            def out_proj(chunks, factor):
                with loop(v, OUT_PAIRS, *at_.steps(chunks), (own, 2)) as i:
                    for banks in range(2):
                        split_lo(chunks)
                        residual_panel(banks, chunks, i * 8 + MC * banks, factor)

            def ffn(last=False):
                with loop(v, FFN_PAIRS, *at_.steps(K_CH), (panels_h, 1)) as i:
                    split_lo(2 * K_CH)
                    at_.skip_panel(0, K_CH)
                    for m in range(MC):
                        v.wait_ge(out_of[0], out_n[0](m + 1 - MC))
                        wait_tile(m, K_CH)
                        V.tensor_tensor(hid[:, m], hid[:, m], ps[:, MC + m, 0:N], ALU.mult).then_inc(out_of[1], 1)
                    out_n[1].add(MC)
                    v.wait_ge(h_hi_ready, panels_h.add())
                    V.tensor_tensor(h_lo[:, bass.ds(i * MC, MC)], hid[:],
                                    h_hi[:, bass.ds(i * MC, MC)].bitcast(F32), ALU.subtract).then_inc(h_ready, 1)
                if not last:
                    out_proj(H_CH, 0.5 / ALPHA)
                    return
                for i in range(2 * OUT_PAIRS):
                    split_lo(H_CH - (i == 2 * OUT_PAIRS - 1))
                    residual_panel(i % 2, H_CH, MC * i, 0.5 / ALPHA)

            def over_tiles(x):
                return x.rearrange("p (a n) -> p a n", a=1).broadcast_to([P, DT, N])

            def layer_norm(k):
                for banks in range(2):
                    v.wait_ge(out_of[banks], out_n[banks]())
                V.tensor_reduce(one_sum[:], y[:].rearrange("p t n -> p n t"), AX, ALU.add).then_inc(ln_partial, 1)
                v.wait_ge(ln_summed, k)
                then(V.tensor_scalar(mean[:], ps[:, 0, 0:N], 1.0 / D, None, ALU.mult))
                V.tensor_tensor(y[:], y[:], over_tiles(mean[:]), ALU.subtract).then_inc(ln_centered, 1)
                v.wait_ge(ln_squared, k)
                V.tensor_reduce(one_sum[:], y_norm[:].rearrange("p t n -> p n t"), AX, ALU.add).then_inc(ln_squares, 1)
                v.wait_ge(ln_std, k)
                then(V.reciprocal(rstd[:], rstd[:]))
                then(V.tensor_tensor(y[:], y[:], over_tiles(rstd[:]), ALU.mult))
                for t in range(DT):
                    ins = V.tensor_scalar(y_norm[:, t], y[:, t], ln_g[:, k - 1, t:t + 1], ln_b[:, k - 1, t:t + 1],
                                          ALU.mult, ALU.add)
                ins.then_inc(ln_out, 1)
                if k < 3:
                    v.wait_ge(x_hi_ready, k + 1)
                    V.tensor_tensor(x_lo[:], y_norm[:], x_hi[:].bitcast(F32), ALU.subtract).then_inc(x_ready, 1)

            def z_pair(page=None):
                split_lo(2 * K_CH, page)
                at_.skip_panel(0, K_CH)
                at_.skip_panel(1, K_CH)

            pages = Count()
            k_in = [Count(), Count()]

            def page_scores(seq):
                def one(j):
                    keys = k_ring[:, j % 2]
                    v.wait_ge(k_landed[j % 2], k_in[j % 2].add(16))
                    q = q_bcast[:, bass.ds(seq, 1)].rearrange("p a e -> p (a e)")
                    then(V.tensor_tensor(keys, keys, q, ALU.mult))
                    dst = scores_flat[:, bass.ds(seq * (SLOTS * 16) + j * 16, 16)]
                    V.tensor_reduce(dst, keys.rearrange("p (g d) -> p g d", d=HD), AX, ALU.add).then_inc(k_free, 1)
                return one

            scores_flat = scores[:].rearrange("p b s c -> p (b s c)")

            def rope():
                for rows, j0, j1 in ((P, 0, PT), (B, PT, PT + 1)):
                    w = j1 - j0
                    x = qk_tok[0:rows, j0:j1].rearrange("p j (g d) -> p j g d", d=HD)
                    x1, x2 = x[:, :, :, 0:ROT], x[:, :, :, ROT:2 * ROT]
                    cos, sin = (rope_cs[0:rows, f, j0:j1].rearrange("p j (a r) -> p j a r", a=1)
                                .broadcast_to([rows, w, 16, ROT]) for f in range(2))
                    t = [rope_t[0:rows, k, 0:w] for k in range(4)]
                    V.tensor_tensor(t[0], x1, cos, ALU.mult)
                    V.tensor_tensor(t[1], x2, sin, ALU.mult)
                    V.tensor_tensor(t[2], x2, cos, ALU.mult)
                    then(V.tensor_tensor(t[3], x1, sin, ALU.mult))
                    V.tensor_tensor(x1, t[0], t[1], ALU.subtract)
                    ins = V.tensor_tensor(x2, t[2], t[3], ALU.add)
                    if j0 == 0:
                        then(ins)
                ins.then_inc(roped, 1)

            v.sem_inc(w_lo_ready, 2)
            v.sem_inc(k_free, 2)
            v.sem_inc(h_ready, 1)
            v.wait_ge(x_hi_ready, 1)
            V.tensor_tensor(x_lo[:], y_norm[:], x_hi[:].bitcast(F32), ALU.subtract).then_inc(x_ready, 1)
            v.wait_ge(const_in, CONSTS)
            v.wait_ge(made, MADE)
            for c in range(2):
                V.tensor_tensor(lam_prod[:, c:c + 1], lam_in[:, 2 * c:2 * c + 1], lam_in[:, 2 * c + 1:2 * c + 2],
                                ALU.mult).then_inc(lam_prod_ready, 1)
            v.wait_ge(lam_exp, 1)
            then(V.tensor_tensor(lam[:, 2:3], lam[:, 1:2], lam[:, 0:1], ALU.subtract))
            then(V.tensor_scalar(lam[:, 2:3], lam[:, 2:3], -LAMBDA_INIT, None, ALU.add))
            V.tensor_scalar(neg_eye[:], ident[0:B, 0:B], -NEG, NEG, ALU.mult, ALU.add)
            then(V.tensor_scalar(subln[:], subln[:], 1.0 - LAMBDA_INIT, None, ALU.mult))
            split_lo(1)
            ffn()
            layer_norm(1)
            z_pair()
            v.wait_ge(tok_ready, 3)
            rope()
            v.wait_ge(roped, 1)
            V.tensor_copy(q_s[:], qk_tok[0:B, PT]).then_inc(q_kept, 1)
            z_pair()
            v.wait_ge(qb_landed, 16 * B)
            z_pair(page_scores(0))
            v.wait_ge(tok_ready, 6)
            rope()
            v.wait_ge(roped, 2)
            v.wait_ge(q_stored, 16)
            then(V.tensor_tensor(q_s[:], q_s[:], qk_tok[0:B, PT], ALU.mult))
            V.memset(scores[:, :, PAGES], NEG)
            then(V.tensor_reduce(s_tmp[:, 0], q_s[:].rearrange("p (g d) -> p g d", d=HD), AX, ALU.add))
            new = scores[0:B, :, PAGES]
            then(V.tensor_tensor(new, s_tmp[:, 0:1].broadcast_to([B, B, 16]),
                                 ident[0:B, 0:B].rearrange("p (b a) -> p b a", a=1).broadcast_to([B, B, 16]), ALU.mult))
            then(V.tensor_tensor(new, new,
                                 neg_eye[:].rearrange("p (b a) -> p b a", a=1).broadcast_to([B, B, 16]), ALU.add))

            def prompt_max(h):
                v.wait_ge(sc_done, h + 1)
                s = h % 2
                for c in range(2):
                    V.scalar_tensor_tensor(prob[:, s, c].rearrange("p b k -> p (b k)"), ps[:, 2 * s + c, 0:3 * P], SCALE,
                                           mask[:].rearrange("p b k -> p (b k)"), ALU.mult, ALU.add).then_inc(sc_masked, 1)
                v.wait_ge(sc_masked, 2 * (h + 1))
                for c in range(2):
                    V.tensor_reduce(stats[:, s, 2 * c:2 * c + 1], prob[:, s, c, 0], AX, ALU.max)
                    ins = V.tensor_reduce(stats[:, s, 2 * c + 1:2 * c + 2],
                                          prob[:, s, c, 1:3].rearrange("p b k -> p (b k)"), AX, ALU.max)
                then(ins)
                V.tensor_scalar(stats[:, s, 4:8], stats[:, s, 0:4], -1.0, None, ALU.mult).then_inc(sc_max, 1)

            def prompt_attn(h):
                v.wait_ge(sc_exp, 4 * (h + 1))
                s = h % 2
                then(V.reciprocal(stats[:, s, 12:16], stats[:, s, 8:12]))
                then(V.tensor_scalar(stats[:, s, 14:16], stats[:, s, 14:16], lam[:, 2:3], None, ALU.mult))
                if h >= 1:
                    v.wait_ge(at_turned, h)
                parts = ((0, slice(0, 1)), (1, slice(1, 3)))
                for j, b in parts:
                    ins = V.tensor_scalar(attn[:, b], prob[:, s, 0, b], stats[:, s, 12 + j:13 + j], None, ALU.mult)
                then(ins)
                for j, b in parts:
                    ins = V.scalar_tensor_tensor(attn[:, b].rearrange("p b k -> p (b k)"),
                                                 prob[:, s, 1, b].rearrange("p b k -> p (b k)"),
                                                 stats[:, s, 14 + j:15 + j],
                                                 attn[:, b].rearrange("p b k -> p (b k)"), ALU.mult, ALU.add)
                ins.then_inc(at_ready, 1)

            for h in range(HEADS):
                prompt_max(h)
                if h >= 1:
                    prompt_attn(h - 1)
            prompt_attn(HEADS - 1)

            with loop(v, C_PAIRS, *at_.steps(K_CH), (k_in[0], 64), (k_in[1], 64), (own, PAGES)) as i:
                z_pair(page_scores(i + 1))
            for banks in range(2):
                v.wait_ge(out_of[banks], out_n[banks]())
            V.memset(u_pad[:, :, 0:2], 0.0)
            V.tensor_tensor(u_pad[:, :, 2:2 + T], z_c[:, 1, :, 0:T], z_c[:, 2, :, 0:T], ALU.mult)
            then(V.tensor_tensor(u_s[:], z_c[:, 1, :, T:N], z_c[:, 2, :, T:N], ALU.mult))
            V.tensor_copy(conv_new[:, :, :, 0], conv_state[:, :, :, 1]).then_inc(conv_new_ready, 1)
            V.tensor_copy(conv_new[:, :, :, 1], u_s[:]).then_inc(conv_new_ready, 1)
            taps = [conv_state[:, :, :, 0], conv_state[:, :, :, 1], u_s[:]]
            for j in range(3):
                ins = V.tensor_tensor(conv_t[:, j], taps[j],
                                      conv_w[:, j].rearrange("p (t a) -> p t a", a=1).broadcast_to([P, AT, B]), ALU.mult)
            for t in range(AT):
                ins = V.tensor_scalar(conv_o[:, t, 0:T], u_pad[:, t, 0:T], conv_w[:, 0, t:t + 1], None, ALU.mult)
            then(ins)
            for j in (1, 2):
                for t in range(AT):
                    ins = V.scalar_tensor_tensor(conv_o[:, t, 0:T], u_pad[:, t, j:j + T], conv_w[:, j, t:t + 1],
                                                 conv_o[:, t, 0:T], ALU.mult, ALU.add)
                then(ins)
            then(V.tensor_tensor(conv_t[:, 0], conv_t[:, 0], conv_t[:, 1], ALU.add))
            then(V.tensor_tensor(conv_o[:, :, T:N], conv_t[:, 0], conv_t[:, 2], ALU.add))
            V.tensor_tensor(conv_o[:], conv_o[:], z_c[:, 0], ALU.mult).then_inc(conv_done, 1)
            v.wait_ge(conv_hi, 1)
            V.tensor_tensor(yc_lo[:], conv_o[:], yc_hi[:].bitcast(F32), ALU.subtract).then_inc(yc_ready, 1)

            with loop(v, G_PAIRS, *at_.steps(K_CH), (k_in[0], 64), (k_in[1], 64), (own, PAGES)) as i:
                z_pair(page_scores(i + (1 + C_PAIRS)))

            def gate_tile(c, t):
                return sig[:, c, bass.ds(t, 1)].rearrange("p a n -> p (a n)")

            for banks in range(2):
                v.wait_ge(out_of[banks], out_n[banks]())
            with loop(v, OUT_PAIRS, *at_.steps(A_CH)) as i:
                for banks in range(2):
                    split_lo(A_CH)
                    for m in range(MC):
                        wait_tile(m, A_CH)
                        g = gate_tile(1, i * 8 + (MC * banks + m))
                        V.tensor_tensor(g, g, ps[:, 4 * banks + m, 0:N], ALU.mult).then_inc(out_of[banks], 1)
                        out_n[banks].add()
            V.tensor_reduce(s_max[:].rearrange("p (b c) -> p b c", b=B), scores[:].rearrange("p b s c -> p b c s"),
                            AX, ALU.max).then_inc(ss_max1, 1)
            v.wait_ge(ss_turned, 1)
            then(V.tensor_reduce(s_col[:], ps[:, 0, 0:P], AX, ALU.max))
            V.tensor_scalar(s_diag[:], ident[:], s_col[:], None, ALU.mult).then_inc(ss_diag, 1)
            v.wait_ge(ss_bcast, 1)
            top_score = ps[:, 1, 0:P].rearrange("p (b a c) -> p b a c", b=B, a=1).broadcast_to([P, B, SLOTS, 16])
            V.tensor_tensor(scores[:], scores[:], top_score, ALU.subtract).then_inc(ss_shift, 1)
            v.wait_ge(ss_exp, 1)
            V.tensor_reduce(s_max[:].rearrange("p (b c) -> p b c", b=B), scores[:].rearrange("p b s c -> p b c s"),
                            AX, ALU.add).then_inc(ss_sums, 1)
            v.wait_ge(ss_den, 1)
            then(V.reciprocal(s_rec[:], ps[:, 2, 0:P]))
            rec = s_rec[:].rearrange("p (b a h c) -> p b a h c", b=B, a=1, c=2)
            then(V.tensor_scalar(rec[:, :, 0, :, 1], rec[:, :, 0, :, 1], lam[:, 2:3], None, ALU.mult))
            e = scores[:].rearrange("p b s (h c) -> p b s h c", c=2)
            V.tensor_tensor(s_attn[:], e[:, :, :, :, 0], rec[:, :, :, :, 0].broadcast_to([P, B, SLOTS, HEADS]), ALU.mult)
            then(V.tensor_tensor(s_attn2[:], e[:, :, :, :, 1], rec[:, :, :, :, 1].broadcast_to([P, B, SLOTS, HEADS]), ALU.mult))
            V.tensor_tensor(s_attn[:], s_attn[:], s_attn2[:], ALU.add).then_inc(ss_attn, 1)
            v.wait_ge(o_std, 2)
            then(V.reciprocal(o_sq[:], o_sq[:]))
            V.scalar_tensor_tensor(o_all[:].rearrange("p h n -> p (h n)"), o_all[:].rearrange("p h n -> p (h n)"),
                                   subln[:], o_sq[:].rearrange("p h n -> p (h n)"), ALU.mult, ALU.mult).then_inc(o_scaled, 1)
            v.wait_ge(o_hi_ready, 1)
            V.tensor_tensor(o_lo[:], o_all[:], o_hi[:].bitcast(F32), ALU.subtract).then_inc(o_split, 1)
            panels_m = Count()
            with loop(v, OUT_PAIRS, *at_.steps(A_CH), (panels_m, 1)) as i:
                for banks in range(2):
                    split_lo(A_CH)
                    for m in range(MC):
                        wait_tile(m, A_CH)
                        g = gate_tile(0, i * 8 + (MC * banks + m))
                        V.tensor_tensor(g, g, ps[:, 4 * banks + m, 0:N], ALU.mult).then_inc(out_of[banks], 1)
                        out_n[banks].add()
                    v.wait_ge(out_of[banks], out_n[banks]())
                    four = bass.ds(i * 8 + MC * banks, MC)
                    V.tensor_tensor(sig[:, 1, four], sig[:, 1, four], sig[:, 0, four], ALU.add).then_inc(m_sum, 1)
                v.wait_ge(m_hi_ready, panels_m.add())
                V.tensor_tensor(m_lo[:, bass.ds(i * 8, 8)], sig[:, 1, bass.ds(i * 8, 8)],
                                m_hi[:, bass.ds(i * 8, 8)].bitcast(F32), ALU.subtract).then_inc(m_ready, 1)
            out_proj(K_CH, 1.0 / ALPHA)
            layer_norm(2)
            ffn(last=True)
            layer_norm(3)


def rope_tables():
    inv = np.power(np.float32(500000.0), -np.arange(0, 2 * ROT, 2, dtype=np.float32) / np.float32(2 * ROT))
    pos = np.full((P, 3), PAGE * PAGES, np.float32)
    for j in range(PT):
        pos[:, j] = np.arange(j * P, (j + 1) * P)
    ang = (pos[:, :, None] * inv.astype(np.float32)).astype(np.float32)
    return np.stack([np.cos(ang), np.sin(ang)], axis=1).astype(np.float32)


_PLAIN = ["cache_k", "cache_v", "ffn1_w_gate", "ffn1_w_up", "ffn1_w_down", "w_in", "w_attn_out", "w_conv_out",
          "w_o", "ffn2_w_gate", "ffn2_w_up", "ffn2_w_down"]
_OUTS = {"y_t": (D, N), "k_prompt": (T, DC), "v_prompt": (T, DC), "k_sample": (B, DC), "v_sample": (B, DC),
         "conv_prompt_t": (DC, 2), "conv_sample_t": (DC, B, 2)}


def kernel(**inputs):
    import concourse.bacc as bacc
    from concourse.bass_utils import run_bass_kernel_spmd

    x = {k: np.asarray(v) for k, v in inputs.items()}
    feats = lambda v, t: v.reshape(-1, t, P).transpose(2, 0, 1)
    arrays = {k: x[k] for k in _PLAIN}
    arrays |= {
        "x_prompt_t": x["x_prompt"][0].T,
        "x_sample_t": x["x_sample"][:, 0].T,
        "page_table": x["page_table"].reshape(1, -1),
        "ln_g": feats(x["ln_g"], DT), "ln_b": feats(x["ln_b"], DT), "conv_w": feats(x["conv_w"], AT),
        "state_conv": x["state_conv"][0].reshape(B, 2, AT, P).transpose(3, 2, 0, 1),
        "rope": rope_tables(),
        "subln_g": x["subln_g"].reshape(P, 1),
        "lambdas": np.concatenate([x["lambda_" + k] for k in ("q1", "k1", "q2", "k2")]).T,
    }
    nc = bacc.Bacc("TRN2", target_bir_lowering=False, num_devices=1)
    feed, args, outs = {}, {}, {}
    for name, v in arrays.items():
        v = np.ascontiguousarray(v)
        feed["in_" + name] = v
        args[name] = nc.dram_tensor("in_" + name, v.shape, mybir.dt.from_np(v.dtype), kind="ExternalInput").ap()
    for name, shape in _OUTS.items():
        outs[name] = nc.dram_tensor("out_" + name, shape, F32, kind="ExternalOutput").ap()
    program(nc, args, outs)
    r = run_bass_kernel_spmd(nc, [feed], core_ids=[0]).results[0]
    r = {k: r["out_" + k] for k in _OUTS}
    yt = r["y_t"].T
    heads = (HEADS, VD)
    return (yt[:T].reshape(1, T, D), yt[T:].reshape(B, 1, D),
            r["k_prompt"].reshape(1, 1, T, *heads), r["v_prompt"].reshape(1, 1, T, *heads),
            r["conv_prompt_t"].T.reshape(1, 1, 2, DC),
            r["k_sample"].reshape(1, B, 1, *heads), r["v_sample"].reshape(1, B, 1, *heads),
            r["conv_sample_t"].transpose(1, 2, 0).reshape(1, B, 2, DC))
```

```python
from contextlib import ExitStack, contextmanager

import numpy as np
import concourse.bass as bass
from concourse import mybir

ALU = mybir.AluOpType
ACT = mybir.ActivationFunctionType
F32 = mybir.dt.float32
F32R = mybir.dt.float32r
I32 = mybir.dt.int32
AX = mybir.AxisListType.X

P = 128
D = 2048
T = 256
B = 8
N = T + B
F = 5632
HEADS, HD, VD = 8, 64, 128
DC = 1024
PAGE, PAGES = 128, 8
DT, FT, AT = D // P, F // P, DC // P
KC, MC = 2, 4
RING = 4
LEAD = 3
WC = MC * P
ALPHA = 2.0 ** 0.25
LN_EPS = 1e-5
LAMBDA_INIT = 0.8 - 0.6
SCALE = HD ** -0.5
NEG = -1e30
ROT = 8
SLOTS = PAGES + 1
PT = 2


class Count:

    def __init__(self, n=0):
        self.n, self.term = n, 0

    def __call__(self, ahead=0):
        return self.term + (self.n + ahead)

    def add(self, by=1):
        self.n += by
        return self()


@contextmanager
def loop(eng, times, *steps):
    with eng.Fori(0, times) as i:
        starts = [c.n for c, _ in steps]
        for c, s in steps:
            c.term = i * s
        yield i
        for (c, s), n in zip(steps, starts):
            assert c.n == n + s, (c.n, n, s)
    for (c, s), n in zip(steps, starts):
        c.term, c.n = 0, n + times * s


class Progress:

    def __init__(self):
        self.split = Count()
        self.landed = [Count() for _ in range(RING)]
        self.tiles = Count()
        self.chunks = Count(RING)
        self.out = [Count(MC), Count(MC)]

    def steps(self, chunks):
        return ((self.split, 2 * chunks), *((slot, 16 * 2 * chunks // RING) for slot in self.landed),
                (self.tiles, 2 * (MC - 1)), (self.chunks, 2 * chunks), (self.out[0], MC), (self.out[1], MC))

    def skip_panel(self, banks, chunks):
        self.tiles.add(MC - 1)
        self.chunks.add(chunks)
        self.out[banks].add(MC)


def program(nc, a, out):
    with ExitStack() as ctx:
        def sem(name):
            return ctx.enter_context(nc.semaphore(name))

        top = nc.sbuf_base
        end = nc.sbuf_usable_end

        def at(name, shape, dt=F32, offset=None):
            nonlocal top
            size = int(np.prod(shape[1:])) * 4
            if offset is None:
                top = -(-top // 32) * 32
                offset, top = top, top + size
            assert offset + size <= end, (name, offset, size, end)
            return nc.alloc_sbuf_tensor_at(name, shape, dt, offset=offset)

        TILE = N * 4
        x_at = (top + 31) // 32 * 32
        x_hi = at("x_hi", [P, DT, N], F32R)
        x_lo = at("x_lo", [P, DT, N], F32R)
        y = at("y", [P, DT, N], F32, x_at)
        y_norm = at("y_norm", [P, DT, N], F32, x_at + DT * TILE)
        w_raw = at("w_raw", [P, RING, KC, WC])
        w_hi = at("w_hi", [P, RING, KC, WC], F32R)
        w_lo = at("w_lo", [P, RING, KC, WC], F32R)
        ident = at("ident", [P, P])
        ones = at("ones", [P, P])
        mask = at("mask", [P, 3, P])
        ln_g = at("ln_g", [P, 3, DT])
        ln_b = at("ln_b", [P, 3, DT])
        conv_w = at("conv_w", [P, 3, AT])
        conv_state = at("conv_state", [P, AT, B, 2])
        rope_cs = at("rope_cs", [P, 2, 3, ROT])
        subln = at("subln", [P, 1])
        lam_in = at("lam_in", [HD, 4])
        lam_prod = at("lam_prod", [HD, 2])
        lam = at("lam", [P, 4])
        page_ids = at("page_ids", [1, B * PAGES], I32)
        neg_eye = at("neg_eye", [B, B])
        one_sum = at("one_sum", [P, N])
        mean = at("mean", [P, N])
        rstd = at("rstd", [P, N])
        eps = at("eps", [P, 2])
        area = (top + 31) // 32 * 32

        h_hi = at("h_hi", [P, FT, N], F32R, area)
        h_lo = at("h_lo", [P, FT, N], F32R, area + FT * TILE)
        hid = at("hid", [P, MC, N], F32, area + 2 * FT * TILE)

        top = area
        o_all = at("o_all", [P, HEADS, N])
        scores = at("scores", [P, B, SLOTS, 2 * HEADS])
        k_ring = at("k_ring", [P, 2, DC])
        qb_at = (top + 31) // 32 * 32
        q_bcast = at("q_bcast", [P, B, DC])
        m_hi = at("m_hi", [P, DT, N], F32R, qb_at)
        m_lo = at("m_lo", [P, DT, N], F32R, qb_at + DT * TILE)
        v_s = at("v_s", [B, DC])
        assert 2 * DT * TILE <= (B + 1) * DC * 4
        early = (top + 31) // 32 * 32
        z_q = at("z_q", [P, AT, N])
        z_k = at("z_k", [P, AT, N])
        zv_at = (top + 31) // 32 * 32
        z_v = at("z_v", [P, AT, N])
        qk_tok = at("qk_tok", [P, 3, DC])
        v_tok = at("v_tok", [P, PT, DC])
        q_s = at("q_s", [B, DC])
        rope_at = (top + 31) // 32 * 32
        rope_t = at("rope_t", [P, 4, PT, 2 * HEADS, ROT])
        stats = at("stats", [P, 2, 16])
        s_tmp = at("s_tmp", [B, 2, 2 * HEADS])
        prob = at("prob", [P, 2, 2, 3, P], F32, zv_at)
        attn = at("attn", [P, 3, P], F32, zv_at + 6144)
        attn_t = at("attn_t", [P, 3, P], F32, rope_at)
        top = early
        c_at = early
        z_c = at("z_c", [P, 3, AT, N])
        sig = at("sig", [P, 2, DT, N])
        sig_at = early + 3 * AT * TILE
        u_pad = at("u_pad", [P, AT, 2 + T], F32, sig_at)
        u_s = at("u_s", [P, AT, B], F32, sig_at + 9216)
        conv_o = at("conv_o", [P, AT, N], F32, sig_at + 10240)
        conv_t = at("conv_t", [P, 3, AT, B], F32, sig_at + 19456)
        conv_new = at("conv_new", [P, AT, B, 2], F32, sig_at + 20480)
        yc_hi = at("yc_hi", [P, AT, N], F32R, c_at + AT * TILE)
        yc_lo = at("yc_lo", [P, AT, N], F32R, c_at + 2 * AT * TILE)
        o_hi = at("o_hi", [P, AT, N], F32R, c_at)
        o_lo = at("o_lo", [P, AT, N], F32R, c_at + AT * TILE)
        o_sq = at("o_sq", [P, AT, N], F32, c_at + 2 * AT * TILE)
        kr_at = qb_at - 2 * DC * 4
        s_max = at("s_max", [P, P], F32, kr_at)
        s_diag = at("s_diag", [P, P], F32, kr_at + 512)
        s_rec = at("s_rec", [P, P], F32, kr_at + 1024)
        s_attn = at("s_attn", [P, B, SLOTS, HEADS], F32, kr_at + 1536)
        s_attn2 = at("s_attn2", [P, B, SLOTS, HEADS], F32, kr_at + 4096)
        s_col = at("s_col", [P, 1], F32, kr_at + 7168)
        s_weights = at("s_weights", [P, B, PAGES, 2, HEADS], F32R, qb_at)
        s_sums = at("s_sums", [2 * HEADS, DC], F32, qb_at + 4096)
        own_head = at("own_head", [2 * HEADS, HEADS], F32, qb_at + 8192)

        ps = ctx.enter_context(nc.psum_tensor("ps", [P, 8, 512], F32))

        const_in = sem("const_in")
        page_ids_in = sem("page_ids_in")
        x_in = sem("x_in")
        made = sem("made")
        w_landed = [sem(f"w_landed{i}") for i in range(RING)]
        w_hi_ready = sem("w_hi_ready")
        w_lo_ready = sem("w_lo_ready")
        w_used = sem("w_used")
        tile_done = sem("tile_done")
        out_of = [sem("out_of_banks0"), sem("out_of_banks1")]
        x_hi_ready = sem("x_hi_ready")
        x_ready = sem("x_ready")
        h_hi_ready = sem("h_hi_ready")
        h_ready = sem("h_ready")
        dve_step = sem("dve_step")
        lam_prod_ready = sem("lam_prod_ready")
        lam_sum = sem("lam_sum")
        lam_exp = sem("lam_exp")
        ln_partial = sem("ln_partial")
        ln_summed = sem("ln_summed")
        ln_centered = sem("ln_centered")
        ln_squared = sem("ln_squared")
        ln_squares = sem("ln_squares")
        ln_var = sem("ln_var")
        ln_std = sem("ln_std")
        ln_out = sem("ln_out")
        turned = sem("turned")
        tok_ready = sem("tok_ready")
        roped = sem("roped")
        q_kept = sem("q_kept")
        back = sem("back")
        back_ready = sem("back_ready")
        q_stored = sem("q_stored")
        qb_landed = sem("qb_landed")
        k_landed = [sem("k_landed0"), sem("k_landed1")]
        k_free = sem("k_free")
        sc_done = sem("sc_done")
        sc_masked = sem("sc_masked")
        sc_max = sem("sc_max")
        sc_exp = sem("sc_exp")
        at_ready = sem("at_ready")
        at_turned = sem("at_turned")
        att_ready = sem("att_ready")
        pv_done = sem("pv_done")
        o_ready = sem("o_ready")
        conv_done = sem("conv_done")
        conv_new_ready = sem("conv_new_ready")
        conv_hi = sem("conv_hi")
        yc_ready = sem("yc_ready")
        ss_max1 = sem("ss_max1")
        ss_turned = sem("ss_turned")
        ss_diag = sem("ss_diag")
        ss_bcast = sem("ss_bcast")
        ss_shift = sem("ss_shift")
        ss_exp = sem("ss_exp")
        ss_sums = sem("ss_sums")
        ss_den = sem("ss_den")
        ss_attn = sem("ss_attn")
        pv_weights_hi = sem("pv_weights_hi")
        pv_weights = sem("pv_weights")
        seq_out = sem("seq_out")
        seq_turned = sem("seq_turned")
        seqs_out = sem("seqs_out")
        o_square = sem("o_square")
        o_sumsq = sem("o_sumsq")
        o_std = sem("o_std")
        o_scaled = sem("o_scaled")
        o_hi_ready = sem("o_hi_ready")
        o_split = sem("o_split")
        m_sum = sem("m_sum")
        m_hi_ready = sem("m_hi_ready")
        m_ready = sem("m_ready")
        kv_stored = sem("kv_stored")
        conv_stored = sem("conv_stored")
        y_stored = sem("y_stored")

        q_scratch = nc.dram_tensor("q_scratch", [B, DC], F32, kind="Internal").ap()
        block = ctx.enter_context(nc.Block())

        K_CH, H_CH, A_CH = DT // KC, FT // KC, AT // KC
        FFN_PAIRS = F // WC
        OUT_PAIRS = D // WC // 2
        C_PAIRS = 3 * DC // (2 * WC)
        G_PAIRS = 2 * D // (2 * WC)
        CONSTS, MADE = 16 * 7, 8
        assert KC * WC == DC and A_CH == B // 2

        @block.sync
        def _(sp):
            n = Count()
            pages = Count()

            def chunk(w, k0, col):
                sp.wait_ge(w_lo_ready, n.add())
                s = (n.n - 1) % RING
                src = w[k0 * P:(k0 + KC) * P, bass.ds(col, WC)].rearrange("(k p) n -> p k n", p=P)
                sp.dma_start(w_raw[:, s], src).then_inc(w_landed[s], 16)

            def ffn(gate, up, down):
                with loop(sp, FFN_PAIRS, (n, 2 * K_CH)) as i:
                    for w in (gate, up):
                        for c in range(K_CH):
                            chunk(w, KC * c, i * WC)
                out_proj(down, H_CH)

            def out_pair(w, chunks, i, part=slice(None)):
                for p, c in [(p, c) for p in range(2) for c in range(chunks)][part]:
                    chunk(w, KC * c, i * (2 * WC) + p * WC)

            def out_proj(w, chunks):
                with loop(sp, OUT_PAIRS, (n, 2 * chunks)) as i:
                    out_pair(w, chunks, i)

            def page_numbers(seq):
                return nc.values_load_multi_w_load_instructions(
                    page_ids[0:1, bass.ds(seq * PAGES, PAGES)], engines=[mybir.EngineType.SP],
                    min_val=0, max_val=a["cache_k"].shape[1] - 1)[1]

            def page(cache, p, dst):
                return sp.dma_start(dst, cache[0, bass.ds(p, 1)].rearrange("a k h e -> (a k) (h e)"))

            def w_in_pair(i, seq=None):
                ids = None if seq is None else page_numbers(seq)
                for p in range(2):
                    for c in range(K_CH):
                        chunk(a["w_in"][0], KC * c, i * (2 * WC) + p * WC)
                        if seq is not None and c % 2 == 1:
                            j = (p * K_CH + c) // 2
                            sp.wait_ge(k_free, pages.add())
                            page(a["cache_k"], ids[j], k_ring[:, j % 2]).then_inc(k_landed[j % 2], 16)

            sp.dma_start(y_norm[:, :, 0:T], a["x_prompt_t"].rearrange("(t p) n -> p t n", p=P)).then_inc(x_in, 16)
            sp.dma_start(y_norm[:, :, T:N], a["x_sample_t"].rearrange("(t p) n -> p t n", p=P)).then_inc(x_in, 16)
            sp.dma_start(page_ids[:], a["page_table"]).then_inc(page_ids_in, 16)
            ffn(a["ffn1_w_gate"][0], a["ffn1_w_up"][0], a["ffn1_w_down"][0])
            w_in_pair(0)
            sp.wait_ge(page_ids_in, 16)
            w_in_pair(1)
            sp.wait_ge(q_kept, 1)
            sp.dma_start(q_scratch, q_s[:]).then_inc(q_stored, 16)
            sp.wait_ge(q_stored, 16)
            for b in range(B):
                sp.dma_start(q_bcast[:, b], q_scratch[b:b + 1].broadcast_to([P, DC])).then_inc(qb_landed, 16)
            with loop(sp, B, (n, 2 * K_CH), (pages, PAGES)) as i:
                w_in_pair(i + 2, i)

            def v_pages(b):
                ids = page_numbers(b)
                for j in range(PAGES):
                    sp.wait_ge(w_lo_ready, n.add())
                    s = (n.n - 1) % RING
                    page(a["cache_v"], ids[j], w_raw[:, s].rearrange("p k n -> p (k n)")).then_inc(w_landed[s], 16)

            out_pair(a["w_conv_out"][0], A_CH, 0)
            for b in range(B):
                out_pair(a["w_conv_out"][0], A_CH, 1, slice(b, b + 1))
                v_pages(b)
            out_proj(a["w_attn_out"][0], A_CH)
            out_proj(a["w_o"][0], K_CH)
            ffn(a["ffn2_w_gate"][0], a["ffn2_w_up"][0], a["ffn2_w_down"][0])
            sp.wait_ge(ln_out, 3)
            sp.dma_start(out["y_t"].rearrange("(t p) n -> p t n", p=P), y_norm[:]).then_inc(y_stored, 16)
            sp.wait_ge(y_stored, 16)
            sp.wait_ge(kv_stored, 16 * 4)
            sp.wait_ge(conv_stored, 16 * 2)

        @block.gpsimd
        def _(pool):
            nc.gpsimd.memset(ones[:], 1.0).then_inc(made, 1)
            nc.gpsimd.memset(ident[:], 0.0).then_inc(made, 1)
            nc.gpsimd.memset(mask[:], 0.0).then_inc(made, 1)
            nc.gpsimd.memset(eps[:, 0:1], LN_EPS / ALPHA ** 2).then_inc(made, 1)
            nc.gpsimd.memset(eps[:, 1:2], LN_EPS).then_inc(made, 1)
            pool.wait_ge(made, 5)
            nc.gpsimd.affine_select(out=ident[:], in_=ident[:], compare_op=ALU.not_equal, fill=1.0, base=0,
                                    pattern=[[-1, P]], channel_multiplier=1).then_inc(made, 1)
            for j in (0, 2):
                nc.gpsimd.affine_select(out=mask[:, j], in_=mask[:, j], compare_op=ALU.is_ge, fill=NEG, base=0,
                                        pattern=[[-1, P]], channel_multiplier=1).then_inc(made, 1)
            for dst, src in ((ln_g, "ln_g"), (ln_b, "ln_b"), (conv_w, "conv_w"), (conv_state, "state_conv"),
                             (rope_cs, "rope"), (subln, "subln_g"), (lam_in, "lambdas")):
                pool.dma_start(dst[:], a[src]).then_inc(const_in, 16)

        @block.tensor
        def _(pe):
            n = Count()
            uses = [Count(), Count()]

            def panel(banks, hi, lo, chunks, after=None):
                for c in range(chunks):
                    if after is not None and c > 0:
                        after(c - 1)
                    pe.wait_ge(w_lo_ready, n.add() + RING)
                    s = (n.n - 1) % RING
                    for m in range(MC):
                        acc = ps[:, 4 * banks + m, 0:N]
                        if c == 0:
                            pe.wait_ge(out_of[banks], uses[banks].add())
                        for k in range(KC):
                            kt = c * KC + k
                            wh, wl = w_hi[:, s, k, m * P:(m + 1) * P], w_lo[:, s, k, m * P:(m + 1) * P]
                            nc.tensor.matmul(acc, wh, hi[:, kt], start=(kt == 0), stop=False)
                            nc.tensor.matmul(acc, wh, lo[:, kt], start=False, stop=False)
                            mm = nc.tensor.matmul(acc, wl, hi[:, kt], start=False, stop=(kt == chunks * KC - 1))
                        if m == MC - 1:
                            mm.then_inc(w_used, 1)
                        elif c == chunks - 1:
                            mm.then_inc(tile_done, 1)
                if after is not None:
                    after(chunks - 1)

            def pairs(times, hi, lo, chunks):
                with loop(pe, times, (n, 2 * chunks), (uses[0], MC), (uses[1], MC)):
                    for banks in range(2):
                        panel(banks, hi, lo, chunks)

            def pair(hi, lo, chunks):
                for banks in range(2):
                    panel(banks, hi, lo, chunks)

            def ffn(k):
                pairs(FFN_PAIRS, x_hi, x_lo, K_CH)
                pe.wait_ge(h_ready, 1 + FFN_PAIRS * k)
                pairs(OUT_PAIRS, h_hi, h_lo, H_CH)

            def banks_free():
                for banks in range(2):
                    pe.wait_ge(out_of[banks], uses[banks](MC))

            def layer_norm(k):
                banks_free()
                pe.wait_ge(ln_partial, k)
                nc.tensor.matmul(ps[:, 0, 0:N], ones[:], one_sum[:], start=True, stop=True).then_inc(ln_summed, 1)
                pe.wait_ge(ln_squares, k)
                nc.tensor.matmul(ps[:, 1, 0:N], ones[:], one_sum[:], start=True, stop=True).then_inc(ln_var, 1)

            def to_tokens(z):
                for j in range(3):
                    for t in range(AT):
                        w = P if j < PT else B
                        mm = nc.tensor.transpose(ps[0:w, 2 * j + t // 4, (t % 4) * P:(t % 4 + 1) * P],
                                                 z[:, t, j * P:j * P + w], ident[:])
                mm.then_inc(turned, 1)

            def from_tokens():
                for h in range(HEADS):
                    for j in range(PT):
                        mm = nc.tensor.transpose(ps[:, h // 2, (h % 2) * T + j * P:(h % 2) * T + (j + 1) * P],
                                                 qk_tok[:, j, h * VD:(h + 1) * VD], ident[:])
                mm.then_inc(back, 1)

            pe.sem_inc(w_used, RING)
            for banks in range(2):
                pe.sem_inc(out_of[banks], MC)
            pe.wait_ge(made, MADE)
            pe.wait_ge(lam_prod_ready, 2)
            nc.tensor.matmul(ps[:, 7, 0:2], ones[0:HD, :], lam_prod[:], start=True, stop=True).then_inc(lam_sum, 1)
            pe.wait_ge(lam_exp, 1)
            pe.wait_ge(x_ready, 1)
            ffn(1)
            layer_norm(1)
            pe.wait_ge(x_ready, 2)
            pair(x_hi, x_lo, K_CH)
            banks_free()
            to_tokens(z_q)
            pe.wait_ge(roped, 1)
            from_tokens()
            pe.wait_ge(back_ready, 1)
            pairs(2, x_hi, x_lo, K_CH)
            banks_free()
            to_tokens(z_k)
            pe.wait_ge(tok_ready, 6)
            pe.wait_ge(roped, 2)
            from_tokens()
            pe.wait_ge(back_ready, 2)
            to_tokens(z_v)
            pe.wait_ge(tok_ready, 9)

            def prompt_scores(h):
                if h >= 2:
                    pe.wait_ge(sc_masked, 2 * (h - 1))
                for c in range(2):
                    q, k = z_q[c * HD:(c + 1) * HD, h], z_k[c * HD:(c + 1) * HD, h]
                    bank = 2 * (h % 2) + c
                    nc.tensor.matmul(ps[:, bank, 0:P], q[:, 0:P], k[:, 0:P], start=True, stop=True)
                    mm = nc.tensor.matmul(ps[:, bank, P:3 * P], q[:, P:T], k[:, 0:T], start=True, stop=True)
                mm.then_inc(sc_done, 1)

            def prompt_values(h):
                pe.wait_ge(at_ready, h + 1)
                if h >= 1:
                    pe.wait_ge(att_ready, h)
                for b in range(3):
                    mm = nc.tensor.transpose(ps[:, 4, b * P:(b + 1) * P], attn[:, b], ident[:])
                mm.then_inc(at_turned, 1)
                pe.wait_ge(att_ready, h + 1)
                if h >= 1:
                    pe.wait_ge(o_ready, h)
                v = v_tok[:, :, h * VD:(h + 1) * VD]
                nc.tensor.matmul(ps[:, 5, 0:P], v[:, 0], attn_t[:, 0], start=True, stop=True)
                nc.tensor.matmul(ps[:, 5, P:T], v[:, 0], attn_t[:, 1], start=True, stop=False)
                nc.tensor.matmul(ps[:, 5, P:T], v[:, 1], attn_t[:, 2], start=False, stop=True).then_inc(pv_done, 1)

            prompt_scores(0)
            prompt_scores(1)
            for h in range(HEADS):
                prompt_values(h)
                if h + 2 < HEADS:
                    prompt_scores(h + 2)
            pe.wait_ge(o_ready, HEADS)
            pairs(C_PAIRS, x_hi, x_lo, K_CH)
            pairs(G_PAIRS, x_hi, x_lo, K_CH)
            pe.wait_ge(yc_ready, 1)
            banks_free()
            pe.wait_ge(ss_max1, 1)
            nc.tensor.transpose(ps[:, 7, 0:P], s_max[:], ident[:]).then_inc(ss_turned, 1)
            panel(0, yc_hi, yc_lo, A_CH)
            pe.wait_ge(ss_diag, 1)
            nc.tensor.matmul(ps[:, 7, 0:P], ones[:], s_diag[:], start=True, stop=True).then_inc(ss_bcast, 1)
            pe.wait_ge(ss_shift, 1)
            panel(1, yc_hi, yc_lo, A_CH)
            pe.wait_ge(ss_sums, 1)
            pe.wait_ge(out_of[0], uses[0](MC))
            nc.tensor.matmul(ps[:, 0, 0:P], ones[:], s_max[:], start=True, stop=True).then_inc(ss_den, 1)
            pe.wait_ge(ss_attn, 1)
            pe.wait_ge(out_of[1], uses[1](MC))
            pe.wait_ge(pv_weights, 1)

            def page_values(b):
                rest = 4 if b < B // 2 else 0
                if b % (B // 2) == 0:
                    pe.wait_ge(out_of[rest // 4], uses[rest // 4](MC))
                    for h in range(HEADS):
                        nc.tensor.matmul(by_head(b, B // 2)[:, :, h], v_s[:, h * VD:(h + 1) * VD],
                                         s_attn[0:B, b:b + B // 2, PAGES, h],
                                         start=(h == 0), stop=False, skip_group_check=True)
                for j in range(PAGES):
                    pe.wait_ge(w_lo_ready, n.add() + RING)
                    s = (n.n - 1) % RING
                    for w in (w_hi, w_lo):
                        for c in range(KC):
                            mm = nc.tensor.matmul(ps[0:2 * HEADS, rest + c], s_weights[:, b, j].rearrange("p c h -> p (c h)"),
                                                  w[:, s, c], start=(j == 0 and w is w_hi), stop=(j == PAGES - 1 and w is w_lo))
                    mm.then_inc(w_used, 1)

            def by_head(b, seqs=1):
                place = ps[:, 6 if b < B // 2 else 2, b * HEADS:(b + seqs) * HEADS]
                return place.rearrange("p (b h) -> p b h", b=seqs)

            def page_turned(b):
                pe.wait_ge(seq_out, b + 1)
                for h in range(HEADS):
                    mm = nc.tensor.matmul(by_head(b)[:, 0, h:h + 1], s_sums[:, h * VD:(h + 1) * VD], own_head[:, h:h + 1],
                                          start=False, stop=True, skip_group_check=True)
                mm.then_inc(seq_turned, 1)

            for banks in range(2):
                def pages(c):
                    b = A_CH * banks + c
                    if c > 0:
                        page_turned(b - 1)
                    page_values(b)

                panel(banks, yc_hi, yc_lo, A_CH, after=pages)
                page_turned(A_CH * (banks + 1) - 1)
                if banks == 0:
                    pe.wait_ge(seqs_out, 1)
            banks_free()
            pe.wait_ge(o_square, 1)
            sq = o_sq[:].rearrange("p h n -> p (h n)")
            for c in range(5):
                w = min(512, AT * N - 512 * c)
                bank = (c + 4) % 8
                mm = nc.tensor.matmul(ps[:, bank, 0:w], ones[:], sq[:, c * 512:c * 512 + w], start=True, stop=True)
            mm.then_inc(o_sumsq, 1)
            pe.wait_ge(o_split, 1)
            pairs(OUT_PAIRS, o_hi, o_lo, A_CH)
            pe.wait_ge(m_ready, OUT_PAIRS)
            pairs(OUT_PAIRS, m_hi, m_lo, K_CH)
            layer_norm(2)
            pe.wait_ge(x_ready, 3)
            ffn(2)
            layer_norm(3)

        @block.scalar
        def _(sc):
            at_ = Progress()
            n, out_n = at_.split, at_.out
            panels_h = Count()

            def split_hi(times):
                for _ in range(times):
                    s = n.n % RING
                    sc.wait_ge(w_used, n(1))
                    sc.wait_ge(w_landed[s], at_.landed[s].add(16))
                    n.add()
                    nc.scalar.activation(w_hi[:, s], w_raw[:, s], ACT.Copy).then_inc(w_hi_ready, 1)

            def take_out(banks, chunks, func, dst):
                at_.chunks.add(chunks)
                for m in range(MC):
                    if m < MC - 1:
                        sc.wait_ge(tile_done, at_.tiles.add())
                    else:
                        sc.wait_ge(w_used, at_.chunks())
                    nc.scalar.activation(dst(m), ps[:, 4 * banks + m, 0:N], func).then_inc(out_of[banks], 1)
                    out_n[banks].add()

            def ffn(last=False):
                with loop(sc, FFN_PAIRS, *at_.steps(K_CH), (panels_h, 1)) as i:
                    split_hi(K_CH - 1)
                    sc.wait_ge(h_ready, panels_h(1))
                    take_out(0, K_CH, ACT.Silu, lambda m: hid[:, m])
                    split_hi(K_CH + 1)
                    at_.skip_panel(1, K_CH)
                    sc.wait_ge(out_of[1], out_n[1]())
                    nc.scalar.activation(h_hi[:, bass.ds(i * MC, MC)], hid[:], ACT.Copy).then_inc(h_hi_ready, 1)
                    panels_h.add()
                if last:
                    split_hi(2 * H_CH * OUT_PAIRS - LEAD)
                else:
                    only_split(OUT_PAIRS, H_CH)

            def only_split(times, chunks):
                with loop(sc, times, *at_.steps(chunks)):
                    split_hi(2 * chunks)
                    at_.skip_panel(0, chunks)
                    at_.skip_panel(1, chunks)

            def layer_norm(k):
                sc.wait_ge(ln_centered, k)
                nc.scalar.activation(y_norm[:], y[:], ACT.Square).then_inc(ln_squared, 1)
                sc.wait_ge(ln_var, k)
                nc.scalar.activation(rstd[:], ps[:, 1, 0:N], ACT.Sqrt, bias=eps[:, 0:1], scale=1.0 / D).then_inc(ln_std, 1)
                if k < 3:
                    sc.wait_ge(ln_out, k)
                    nc.scalar.activation(x_hi[:], y_norm[:], ACT.Copy).then_inc(x_hi_ready, 1)

            def z_pair(tile, func=ACT.Copy):
                for banks in range(2):
                    split_hi(K_CH - 1)
                    take_out(banks, K_CH, func, lambda m: tile(MC * banks + m))
                    split_hi(1)

            def tokens(*dst):
                k = tokens.n = tokens.n + 1
                sc.wait_ge(turned, k)
                for j, d in enumerate(dst):
                    w = P if j < PT else B
                    src = ps[0:w, 2 * j:2 * j + 2].rearrange("p b n -> p (b n)")
                    nc.scalar.activation(d, src, ACT.Copy).then_inc(tok_ready, 1)
            tokens.n = 0

            def turned_back(k, z):
                sc.wait_ge(back, k)
                nc.scalar.activation(z[:, :, 0:T], ps[:, 0:4].rearrange("p b (h t) -> p (b h) t", h=2),
                                     ACT.Copy).then_inc(back_ready, 1)

            sc.wait_ge(x_in, 32)
            nc.scalar.activation(x_hi[:], y_norm[:], ACT.Copy).then_inc(x_hi_ready, 1)
            sc.wait_ge(lam_sum, 1)
            nc.scalar.activation(lam[:, 0:2], ps[:, 7, 0:2], ACT.Exp).then_inc(lam_exp, 1)
            split_hi(LEAD)
            ffn()
            layer_norm(1)
            z_pair(lambda m: z_q[:, m])
            tokens(qk_tok[:, 0], qk_tok[:, 1], qk_tok[0:B, 2])
            turned_back(1, z_q)
            z_pair(lambda m: z_k[:, m])
            z_pair(lambda m: z_v[:, m])
            sc.wait_ge(q_kept, 1)
            tokens(qk_tok[:, 0], qk_tok[:, 1], qk_tok[0:B, 2])
            turned_back(2, z_k)
            tokens(v_tok[:, 0], v_tok[:, 1], v_s[:])
            sc.wait_ge(tok_ready, 9)
            for dst, src in (("k_prompt", qk_tok[:, 0:PT]), ("v_prompt", v_tok[:])):
                sc.dma_start(out[dst].rearrange("(j p) e -> p j e", p=P), src).then_inc(kv_stored, 16)
            for dst, src in (("k_sample", qk_tok[0:B, 2]), ("v_sample", v_s[:])):
                sc.dma_start(out[dst], src).then_inc(kv_stored, 16)

            def prompt_exp(h):
                sc.wait_ge(sc_max, h + 1)
                s = h % 2
                for c in range(2):
                    for j in range(2):
                        blocks = prob[:, s, c, 0:1] if j == 0 else prob[:, s, c, 1:3]
                        i = 2 * c + j
                        nc.scalar.activation(blocks, blocks, ACT.Exp, bias=stats[:, s, 4 + i:5 + i],
                                             accum_out=stats[:, s, 8 + i:9 + i]).then_inc(sc_exp, 1)

            def prompt_out(h):
                sc.wait_ge(at_turned, h + 1)
                if h >= 1:
                    sc.wait_ge(pv_done, h)
                nc.scalar.activation(attn_t[:], ps[:, 4, 0:3 * P].rearrange("p (b q) -> p b q", b=3),
                                     ACT.Copy).then_inc(att_ready, 1)
                sc.wait_ge(pv_done, h + 1)
                nc.scalar.activation(o_all[:, h, 0:T], ps[:, 5, 0:T], ACT.Copy).then_inc(o_ready, 1)

            for h in range(HEADS):
                prompt_exp(h)
                if h >= 1:
                    prompt_out(h - 1)
            prompt_out(HEADS - 1)

            z_all = z_c[:].rearrange("p c t n -> p (c t) n")
            sig_all = sig[:].rearrange("p c t n -> p (c t) n")
            sc.wait_ge(kv_stored, 16 * 4)
            sc.wait_ge(sc_masked, 2 * HEADS)
            with loop(sc, C_PAIRS, *at_.steps(K_CH)) as i:
                z_pair(lambda m: z_all[:, bass.ds(i * 8 + m, 1)])
            sc.wait_ge(conv_new_ready, 2)
            sc.dma_start(out["conv_prompt_t"].rearrange("(t p) k -> p t k", p=P), u_pad[:, :, T:T + 2]).then_inc(conv_stored, 16)
            sc.dma_start(out["conv_sample_t"].rearrange("(t p) b k -> p t b k", p=P), conv_new[:]).then_inc(conv_stored, 16)
            sc.wait_ge(conv_done, 1)
            nc.scalar.activation(yc_hi[:], conv_o[:], ACT.Copy).then_inc(conv_hi, 1)
            sc.wait_ge(yc_ready, 1)
            sc.wait_ge(conv_stored, 16 * 2)
            with loop(sc, G_PAIRS, *at_.steps(K_CH)) as i:
                z_pair(lambda m: sig_all[:, bass.ds(i * 8 + m, 1)], ACT.Sigmoid)
            split_hi(A_CH)
            sc.wait_ge(ss_shift, 1)
            nc.scalar.activation(scores[:], scores[:], ACT.Exp, scale=SCALE).then_inc(ss_exp, 1)
            split_hi(A_CH)
            sc.wait_ge(ss_attn, 1)
            nc.scalar.activation(s_weights[:, :, :, 0], s_attn[:, :, 0:PAGES], ACT.Copy).then_inc(pv_weights_hi, 1)
            at_.chunks.add(2 * A_CH)
            for b in range(B):
                split_hi(PAGES + (0 if b == 0 else 1))
                sc.wait_ge(w_used, at_.chunks.add(1 + PAGES))
                if b > 0:
                    sc.wait_ge(seq_turned, b)
                bank = 4 if b < B // 2 else 0
                nc.scalar.activation(s_sums[:], ps[0:2 * HEADS, bank:bank + KC].rearrange("p c n -> p (c n)"),
                                     ACT.Copy).then_inc(seq_out, 1)
            split_hi(1)
            for k in range(2 * 2):
                at_.skip_panel(k % 2, 0)
            sc.wait_ge(seqs_out, 2)
            nc.scalar.activation(o_sq[:], o_all[:], ACT.Square).then_inc(o_square, 1)
            sc.wait_ge(o_sumsq, 1)
            sq = o_sq[:].rearrange("p h n -> p (h n)")
            nc.scalar.activation(sq[:, 0:2048], ps[:, 4:8].rearrange("p b n -> p (b n)"), ACT.Sqrt,
                                 bias=eps[:, 1:2], scale=1.0 / VD).then_inc(o_std, 1)
            nc.scalar.activation(sq[:, 2048:], ps[:, 0, 0:AT * N - 2048], ACT.Sqrt,
                                 bias=eps[:, 1:2], scale=1.0 / VD).then_inc(o_std, 1)
            sc.wait_ge(o_scaled, 1)
            nc.scalar.activation(o_hi[:], o_all[:], ACT.Copy).then_inc(o_hi_ready, 1)
            panels_m = Count()
            with loop(sc, OUT_PAIRS, *at_.steps(A_CH), (panels_m, 2)) as i:
                split_hi(2 * A_CH)
                at_.skip_panel(0, A_CH)
                at_.skip_panel(1, A_CH)
                sc.wait_ge(m_sum, panels_m.add(2))
                nc.scalar.activation(m_hi[:, bass.ds(i * 8, 8)], sig[:, 1, bass.ds(i * 8, 8)], ACT.Copy).then_inc(m_hi_ready, 1)
            only_split(OUT_PAIRS, K_CH)
            layer_norm(2)
            ffn(last=True)
            layer_norm(3)

        @block.vector
        def _(v):
            at_ = Progress()
            n, out_n = at_.split, at_.out
            own = Count()
            panels_h = Count()
            V = nc.vector

            def then(ins):
                ins.then_inc(dve_step, 1)
                v.wait_ge(dve_step, own.add())

            def split_lo(times, page=None):
                for _ in range(times):
                    s = n.n % RING
                    v.wait_ge(w_hi_ready, n.add())
                    at_.landed[s].add(16)
                    V.tensor_tensor(w_lo[:, s], w_raw[:, s], w_hi[:, s].bitcast(F32), ALU.subtract).then_inc(w_lo_ready, 1)
                    if page is not None and n.n % 2 == 0:
                        page()

            def wait_tile(m, chunks):
                if m == 0:
                    at_.chunks.add(chunks)
                if m < MC - 1:
                    v.wait_ge(tile_done, at_.tiles.add())
                else:
                    v.wait_ge(w_used, at_.chunks())

            def residual_panel(banks, chunks, t0, factor):
                part = y[:, bass.ds(t0, MC)]
                then(V.tensor_tensor(part, x_hi[:, bass.ds(t0, MC)].bitcast(F32),
                                     x_lo[:, bass.ds(t0, MC)].bitcast(F32), ALU.add))
                for m in range(MC):
                    wait_tile(m, chunks)
                    tile = y[:, bass.ds(t0 + m, 1)].rearrange("p a n -> p (a n)")
                    V.scalar_tensor_tensor(tile, ps[:, 4 * banks + m, 0:N], factor, tile,
                                           ALU.mult, ALU.add).then_inc(out_of[banks], 1)
                    out_n[banks].add()

            def out_proj(chunks, factor):
                with loop(v, OUT_PAIRS, *at_.steps(chunks), (own, 2)) as i:
                    for banks in range(2):
                        split_lo(chunks - 1)
                        residual_panel(banks, chunks, i * 8 + MC * banks, factor)
                        split_lo(1)

            def ffn(last=False):
                with loop(v, FFN_PAIRS, *at_.steps(K_CH), (panels_h, 1)) as i:
                    split_lo(2 * K_CH - 1)
                    at_.skip_panel(0, K_CH)
                    for m in range(MC):
                        v.wait_ge(out_of[0], out_n[0](m + 1 - MC))
                        wait_tile(m, K_CH)
                        V.tensor_tensor(hid[:, m], hid[:, m], ps[:, MC + m, 0:N], ALU.mult).then_inc(out_of[1], 1)
                    out_n[1].add(MC)
                    split_lo(1)
                    v.wait_ge(h_hi_ready, panels_h.add())
                    V.tensor_tensor(h_lo[:, bass.ds(i * MC, MC)], hid[:],
                                    h_hi[:, bass.ds(i * MC, MC)].bitcast(F32), ALU.subtract).then_inc(h_ready, 1)
                if not last:
                    out_proj(H_CH, 0.5 / ALPHA)
                    return
                for i in range(2 * OUT_PAIRS):
                    more = i < 2 * OUT_PAIRS - 1
                    split_lo(H_CH - (1 if more else LEAD))
                    residual_panel(i % 2, H_CH, MC * i, 0.5 / ALPHA)
                    split_lo(1 if more else 0)

            def over_tiles(x):
                return x.rearrange("p (a n) -> p a n", a=1).broadcast_to([P, DT, N])

            def layer_norm(k):
                for banks in range(2):
                    v.wait_ge(out_of[banks], out_n[banks]())
                V.tensor_reduce(one_sum[:], y[:].rearrange("p t n -> p n t"), AX, ALU.add).then_inc(ln_partial, 1)
                v.wait_ge(ln_summed, k)
                then(V.tensor_scalar(mean[:], ps[:, 0, 0:N], 1.0 / D, None, ALU.mult))
                V.tensor_tensor(y[:], y[:], over_tiles(mean[:]), ALU.subtract).then_inc(ln_centered, 1)
                v.wait_ge(ln_squared, k)
                V.tensor_reduce(one_sum[:], y_norm[:].rearrange("p t n -> p n t"), AX, ALU.add).then_inc(ln_squares, 1)
                v.wait_ge(ln_std, k)
                then(V.reciprocal(rstd[:], rstd[:]))
                then(V.tensor_tensor(y[:], y[:], over_tiles(rstd[:]), ALU.mult))
                for t in range(DT):
                    ins = V.tensor_scalar(y_norm[:, t], y[:, t], ln_g[:, k - 1, t:t + 1], ln_b[:, k - 1, t:t + 1],
                                          ALU.mult, ALU.add)
                ins.then_inc(ln_out, 1)
                if k < 3:
                    v.wait_ge(x_hi_ready, k + 1)
                    V.tensor_tensor(x_lo[:], y_norm[:], x_hi[:].bitcast(F32), ALU.subtract).then_inc(x_ready, 1)

            def z_pair(page=None):
                split_lo(2 * K_CH, page)
                at_.skip_panel(0, K_CH)
                at_.skip_panel(1, K_CH)

            k_in = [Count(), Count()]
            k_turn = Count()

            def page_scores(seq):
                def one():
                    j = k_turn.n % PAGES
                    k_turn.add()
                    keys = k_ring[:, j % 2]
                    v.wait_ge(k_landed[j % 2], k_in[j % 2].add(16))
                    q = q_bcast[:, bass.ds(seq, 1)].rearrange("p a e -> p (a e)")
                    then(V.tensor_tensor(keys, keys, q, ALU.mult))
                    dst = scores_flat[:, bass.ds(seq * (SLOTS * 16) + j * 16, 16)]
                    V.tensor_reduce(dst, keys.rearrange("p (g d) -> p g d", d=HD), AX, ALU.add).then_inc(k_free, 1)
                return one

            scores_flat = scores[:].rearrange("p b s c -> p (b s c)")

            def rope():
                for rows, j0, j1 in ((P, 0, PT), (B, PT, PT + 1)):
                    w = j1 - j0
                    x = qk_tok[0:rows, j0:j1].rearrange("p j (g d) -> p j g d", d=HD)
                    x1, x2 = x[:, :, :, 0:ROT], x[:, :, :, ROT:2 * ROT]
                    cos, sin = (rope_cs[0:rows, f, j0:j1].rearrange("p j (a r) -> p j a r", a=1)
                                .broadcast_to([rows, w, 16, ROT]) for f in range(2))
                    t = [rope_t[0:rows, k, 0:w] for k in range(4)]
                    V.tensor_tensor(t[0], x1, cos, ALU.mult)
                    V.tensor_tensor(t[1], x2, sin, ALU.mult)
                    V.tensor_tensor(t[2], x2, cos, ALU.mult)
                    then(V.tensor_tensor(t[3], x1, sin, ALU.mult))
                    V.tensor_tensor(x1, t[0], t[1], ALU.subtract)
                    ins = V.tensor_tensor(x2, t[2], t[3], ALU.add)
                    if j0 == 0:
                        then(ins)
                ins.then_inc(roped, 1)

            v.sem_inc(w_lo_ready, RING)
            v.sem_inc(k_free, 2)
            v.sem_inc(h_ready, 1)
            v.wait_ge(x_hi_ready, 1)
            V.tensor_tensor(x_lo[:], y_norm[:], x_hi[:].bitcast(F32), ALU.subtract).then_inc(x_ready, 1)
            v.wait_ge(const_in, CONSTS)
            v.wait_ge(made, MADE)
            for c in range(2):
                V.tensor_tensor(lam_prod[:, c:c + 1], lam_in[:, 2 * c:2 * c + 1], lam_in[:, 2 * c + 1:2 * c + 2],
                                ALU.mult).then_inc(lam_prod_ready, 1)
            v.wait_ge(lam_exp, 1)
            then(V.tensor_tensor(lam[:, 2:3], lam[:, 1:2], lam[:, 0:1], ALU.subtract))
            then(V.tensor_scalar(lam[:, 2:3], lam[:, 2:3], -LAMBDA_INIT, None, ALU.add))
            V.tensor_scalar(neg_eye[:], ident[0:B, 0:B], -NEG, NEG, ALU.mult, ALU.add)
            then(V.tensor_scalar(subln[:], subln[:], 1.0 - LAMBDA_INIT, None, ALU.mult))
            split_lo(LEAD)
            ffn()
            layer_norm(1)
            z_pair()
            v.wait_ge(tok_ready, 3)
            rope()
            v.wait_ge(roped, 1)
            V.tensor_copy(q_s[:], qk_tok[0:B, PT]).then_inc(q_kept, 1)
            z_pair()
            v.wait_ge(qb_landed, 16 * B)
            z_pair(page_scores(0))
            v.wait_ge(tok_ready, 6)
            rope()
            v.wait_ge(roped, 2)
            v.wait_ge(q_stored, 16)
            then(V.tensor_tensor(q_s[:], q_s[:], qk_tok[0:B, PT], ALU.mult))
            V.memset(scores[:, :, PAGES], NEG)
            then(V.tensor_reduce(s_tmp[:, 0], q_s[:].rearrange("p (g d) -> p g d", d=HD), AX, ALU.add))
            new = scores[0:B, :, PAGES]
            then(V.tensor_tensor(new, s_tmp[:, 0:1].broadcast_to([B, B, 16]),
                                 ident[0:B, 0:B].rearrange("p (b a) -> p b a", a=1).broadcast_to([B, B, 16]), ALU.mult))
            then(V.tensor_tensor(new, new,
                                 neg_eye[:].rearrange("p (b a) -> p b a", a=1).broadcast_to([B, B, 16]), ALU.add))

            def prompt_max(h):
                v.wait_ge(sc_done, h + 1)
                s = h % 2
                for c in range(2):
                    V.scalar_tensor_tensor(prob[:, s, c].rearrange("p b k -> p (b k)"), ps[:, 2 * s + c, 0:3 * P], SCALE,
                                           mask[:].rearrange("p b k -> p (b k)"), ALU.mult, ALU.add).then_inc(sc_masked, 1)
                v.wait_ge(sc_masked, 2 * (h + 1))
                for c in range(2):
                    V.tensor_reduce(stats[:, s, 2 * c:2 * c + 1], prob[:, s, c, 0], AX, ALU.max)
                    ins = V.tensor_reduce(stats[:, s, 2 * c + 1:2 * c + 2],
                                          prob[:, s, c, 1:3].rearrange("p b k -> p (b k)"), AX, ALU.max)
                then(ins)
                V.tensor_scalar(stats[:, s, 4:8], stats[:, s, 0:4], -1.0, None, ALU.mult).then_inc(sc_max, 1)

            def prompt_attn(h):
                v.wait_ge(sc_exp, 4 * (h + 1))
                s = h % 2
                then(V.reciprocal(stats[:, s, 12:16], stats[:, s, 8:12]))
                then(V.tensor_scalar(stats[:, s, 14:16], stats[:, s, 14:16], lam[:, 2:3], None, ALU.mult))
                if h >= 1:
                    v.wait_ge(at_turned, h)
                parts = ((0, slice(0, 1)), (1, slice(1, 3)))
                for j, b in parts:
                    ins = V.tensor_scalar(attn[:, b], prob[:, s, 0, b], stats[:, s, 12 + j:13 + j], None, ALU.mult)
                then(ins)
                for j, b in parts:
                    ins = V.scalar_tensor_tensor(attn[:, b].rearrange("p b k -> p (b k)"),
                                                 prob[:, s, 1, b].rearrange("p b k -> p (b k)"),
                                                 stats[:, s, 14 + j:15 + j],
                                                 attn[:, b].rearrange("p b k -> p (b k)"), ALU.mult, ALU.add)
                ins.then_inc(at_ready, 1)

            for h in range(HEADS):
                prompt_max(h)
                if h >= 1:
                    prompt_attn(h - 1)
            prompt_attn(HEADS - 1)

            with loop(v, C_PAIRS, *at_.steps(K_CH), (k_in[0], 64), (k_in[1], 64), (k_turn, PAGES), (own, PAGES)) as i:
                z_pair(page_scores(i + 1))
            for banks in range(2):
                v.wait_ge(out_of[banks], out_n[banks]())
            V.memset(u_pad[:, :, 0:2], 0.0)
            V.tensor_tensor(u_pad[:, :, 2:2 + T], z_c[:, 1, :, 0:T], z_c[:, 2, :, 0:T], ALU.mult)
            then(V.tensor_tensor(u_s[:], z_c[:, 1, :, T:N], z_c[:, 2, :, T:N], ALU.mult))
            V.tensor_copy(conv_new[:, :, :, 0], conv_state[:, :, :, 1]).then_inc(conv_new_ready, 1)
            V.tensor_copy(conv_new[:, :, :, 1], u_s[:]).then_inc(conv_new_ready, 1)
            taps = [conv_state[:, :, :, 0], conv_state[:, :, :, 1], u_s[:]]
            for j in range(3):
                ins = V.tensor_tensor(conv_t[:, j], taps[j],
                                      conv_w[:, j].rearrange("p (t a) -> p t a", a=1).broadcast_to([P, AT, B]), ALU.mult)
            for t in range(AT):
                ins = V.tensor_scalar(conv_o[:, t, 0:T], u_pad[:, t, 0:T], conv_w[:, 0, t:t + 1], None, ALU.mult)
            then(ins)
            for j in (1, 2):
                for t in range(AT):
                    ins = V.scalar_tensor_tensor(conv_o[:, t, 0:T], u_pad[:, t, j:j + T], conv_w[:, j, t:t + 1],
                                                 conv_o[:, t, 0:T], ALU.mult, ALU.add)
                then(ins)
            then(V.tensor_tensor(conv_t[:, 0], conv_t[:, 0], conv_t[:, 1], ALU.add))
            then(V.tensor_tensor(conv_o[:, :, T:N], conv_t[:, 0], conv_t[:, 2], ALU.add))
            V.tensor_tensor(conv_o[:], conv_o[:], z_c[:, 0], ALU.mult).then_inc(conv_done, 1)
            v.wait_ge(conv_hi, 1)
            V.tensor_tensor(yc_lo[:], conv_o[:], yc_hi[:].bitcast(F32), ALU.subtract).then_inc(yc_ready, 1)

            with loop(v, G_PAIRS, *at_.steps(K_CH), (k_in[0], 64), (k_in[1], 64), (k_turn, PAGES), (own, PAGES)) as i:
                z_pair(page_scores(i + (1 + C_PAIRS)))

            def gate_tile(c, t):
                return sig[:, c, bass.ds(t, 1)].rearrange("p a n -> p (a n)")

            for banks in range(2):
                v.wait_ge(out_of[banks], out_n[banks]())

            def conv_gated(banks, t0, chunks):
                for m in range(MC):
                    wait_tile(m, chunks)
                    g = sig[:, 1, t0 + m]
                    V.tensor_tensor(g, g, ps[:, 4 * banks + m, 0:N], ALU.mult).then_inc(out_of[banks], 1)
                    out_n[banks].add()

            v.wait_ge(k_free, 2 + B * PAGES)
            V.tensor_reduce(s_max[:].rearrange("p (b c) -> p b c", b=B), scores[:].rearrange("p b s c -> p b c s"),
                            AX, ALU.max).then_inc(ss_max1, 1)
            v.wait_ge(ss_turned, 1)
            then(V.tensor_reduce(s_col[:], ps[:, 7, 0:P], AX, ALU.max))
            V.tensor_scalar(s_diag[:], ident[:], s_col[:], None, ALU.mult).then_inc(ss_diag, 1)
            split_lo(A_CH)
            v.wait_ge(ss_bcast, 1)
            top_score = ps[:, 7, 0:P].rearrange("p (b a c) -> p b a c", b=B, a=1).broadcast_to([P, B, SLOTS, 16])
            V.tensor_tensor(scores[:], scores[:], top_score, ALU.subtract).then_inc(ss_shift, 1)
            conv_gated(0, 0, A_CH)
            split_lo(1)
            v.wait_ge(ss_exp, 1)
            V.tensor_reduce(s_max[:].rearrange("p (b c) -> p b c", b=B), scores[:].rearrange("p b s c -> p b c s"),
                            AX, ALU.add).then_inc(ss_sums, 1)
            split_lo(1)
            v.wait_ge(ss_den, 1)
            then(V.reciprocal(s_rec[:], ps[:, 0, 0:P]))
            rec = s_rec[:].rearrange("p (b a h c) -> p b a h c", b=B, a=1, c=2)
            then(V.tensor_scalar(rec[:, :, 0, :, 1], rec[:, :, 0, :, 1], lam[:, 2:3], None, ALU.mult))
            e = scores[:].rearrange("p b s (h c) -> p b s h c", c=2)
            V.tensor_tensor(s_attn[:], e[:, :, :, :, 0], rec[:, :, :, :, 0].broadcast_to([P, B, SLOTS, HEADS]), ALU.mult)
            then(V.tensor_tensor(s_attn2[:], e[:, :, :, :, 1], rec[:, :, :, :, 1].broadcast_to([P, B, SLOTS, HEADS]), ALU.mult))
            V.tensor_tensor(own_head[:], ident[0:2 * HEADS, 0:HEADS], ident[0:2 * HEADS, HEADS:2 * HEADS], ALU.add)
            V.tensor_tensor(s_attn[:], s_attn[:], s_attn2[:], ALU.add).then_inc(ss_attn, 1)
            split_lo(2)
            v.wait_ge(pv_weights_hi, 1)
            V.tensor_tensor(s_weights[:, :, :, 1], s_attn[:, :, 0:PAGES], s_weights[:, :, :, 0].bitcast(F32),
                            ALU.subtract).then_inc(pv_weights, 1)
            conv_gated(1, MC, A_CH)
            def seqs_result(half):
                v.wait_ge(seq_turned, (half + 1) * B // 2)
                b0, b1 = half * B // 2, (half + 1) * B // 2
                V.tensor_copy(o_all[:, :, T + b0:T + b1].rearrange("p h b -> p b h"),
                              ps[:, 6 - 4 * half, b0 * HEADS:b1 * HEADS].rearrange("p (b h) -> p b h", b=B // 2)
                              ).then_inc(seqs_out, 1)

            before = A_CH + (A_CH - 1) * PAGES
            split_lo(before - 1)
            conv_gated(0, 2 * MC, before)
            split_lo(PAGES)
            seqs_result(0)
            split_lo(before)
            conv_gated(1, 3 * MC, PAGES + before)
            split_lo(PAGES + 1)
            at_.chunks.add(PAGES)
            seqs_result(1)
            v.wait_ge(o_std, 2)
            then(V.reciprocal(o_sq[:], o_sq[:]))
            V.scalar_tensor_tensor(o_all[:].rearrange("p h n -> p (h n)"), o_all[:].rearrange("p h n -> p (h n)"),
                                   subln[:], o_sq[:].rearrange("p h n -> p (h n)"), ALU.mult, ALU.mult).then_inc(o_scaled, 1)
            v.wait_ge(o_hi_ready, 1)
            V.tensor_tensor(o_lo[:], o_all[:], o_hi[:].bitcast(F32), ALU.subtract).then_inc(o_split, 1)
            panels_m = Count()
            with loop(v, OUT_PAIRS, *at_.steps(A_CH), (panels_m, 1)) as i:
                for banks in range(2):
                    split_lo(A_CH - 1)
                    for m in range(MC):
                        wait_tile(m, A_CH)
                        g = gate_tile(0, i * 8 + (MC * banks + m))
                        V.tensor_tensor(g, g, ps[:, 4 * banks + m, 0:N], ALU.mult).then_inc(out_of[banks], 1)
                        out_n[banks].add()
                    v.wait_ge(out_of[banks], out_n[banks]())
                    four = bass.ds(i * 8 + MC * banks, MC)
                    V.tensor_tensor(sig[:, 1, four], sig[:, 1, four], sig[:, 0, four], ALU.add).then_inc(m_sum, 1)
                    split_lo(1)
                v.wait_ge(m_hi_ready, panels_m.add())
                V.tensor_tensor(m_lo[:, bass.ds(i * 8, 8)], sig[:, 1, bass.ds(i * 8, 8)],
                                m_hi[:, bass.ds(i * 8, 8)].bitcast(F32), ALU.subtract).then_inc(m_ready, 1)
            out_proj(K_CH, 1.0 / ALPHA)
            layer_norm(2)
            ffn(last=True)
            layer_norm(3)


def rope_tables():
    inv = np.power(np.float32(500000.0), -np.arange(0, 2 * ROT, 2, dtype=np.float32) / np.float32(2 * ROT))
    pos = np.full((P, 3), PAGE * PAGES, np.float32)
    for j in range(PT):
        pos[:, j] = np.arange(j * P, (j + 1) * P)
    ang = (pos[:, :, None] * inv.astype(np.float32)).astype(np.float32)
    return np.stack([np.cos(ang), np.sin(ang)], axis=1).astype(np.float32)


_PLAIN = ["cache_k", "cache_v", "ffn1_w_gate", "ffn1_w_up", "ffn1_w_down", "w_in", "w_attn_out", "w_conv_out",
          "w_o", "ffn2_w_gate", "ffn2_w_up", "ffn2_w_down"]
_OUTS = {"y_t": (D, N), "k_prompt": (T, DC), "v_prompt": (T, DC), "k_sample": (B, DC), "v_sample": (B, DC),
         "conv_prompt_t": (DC, 2), "conv_sample_t": (DC, B, 2)}


def kernel(**inputs):
    import concourse.bacc as bacc
    from concourse.bass_utils import run_bass_kernel_spmd

    x = {k: np.asarray(v) for k, v in inputs.items()}
    feats = lambda v, t: v.reshape(-1, t, P).transpose(2, 0, 1)
    arrays = {k: x[k] for k in _PLAIN}
    arrays |= {
        "x_prompt_t": x["x_prompt"][0].T,
        "x_sample_t": x["x_sample"][:, 0].T,
        "page_table": x["page_table"].reshape(1, -1),
        "ln_g": feats(x["ln_g"], DT), "ln_b": feats(x["ln_b"], DT), "conv_w": feats(x["conv_w"], AT),
        "state_conv": x["state_conv"][0].reshape(B, 2, AT, P).transpose(3, 2, 0, 1),
        "rope": rope_tables(),
        "subln_g": x["subln_g"].reshape(P, 1),
        "lambdas": np.concatenate([x["lambda_" + k] for k in ("q1", "k1", "q2", "k2")]).T,
    }
    nc = bacc.Bacc("TRN2", target_bir_lowering=False, num_devices=1)
    feed, args, outs = {}, {}, {}
    for name, v in arrays.items():
        v = np.ascontiguousarray(v)
        feed["in_" + name] = v
        args[name] = nc.dram_tensor("in_" + name, v.shape, mybir.dt.from_np(v.dtype), kind="ExternalInput").ap()
    for name, shape in _OUTS.items():
        outs[name] = nc.dram_tensor("out_" + name, shape, F32, kind="ExternalOutput").ap()
    program(nc, args, outs)
    r = run_bass_kernel_spmd(nc, [feed], core_ids=[0]).results[0]
    r = {k: r["out_" + k] for k in _OUTS}
    yt = r["y_t"].T
    heads = (HEADS, VD)
    return (yt[:T].reshape(1, T, D), yt[T:].reshape(B, 1, D),
            r["k_prompt"].reshape(1, 1, T, *heads), r["v_prompt"].reshape(1, 1, T, *heads),
            r["conv_prompt_t"].T.reshape(1, 1, 2, DC),
            r["k_sample"].reshape(1, B, 1, *heads), r["v_sample"].reshape(1, B, 1, *heads),
            r["conv_sample_t"].transpose(1, 2, 0).reshape(1, B, 2, DC))
```

```python
from contextlib import ExitStack, contextmanager

import numpy as np
import concourse.bass as bass
from concourse import mybir

ALU = mybir.AluOpType
ACT = mybir.ActivationFunctionType
F32 = mybir.dt.float32
F32R = mybir.dt.float32r
I32 = mybir.dt.int32
AX = mybir.AxisListType.X

P = 128
D = 2048
T = 256
B = 8
N = T + B
F = 5632
HEADS, HD, VD = 8, 64, 128
DC = 1024
PAGE, PAGES = 128, 8
DT, FT, AT = D // P, F // P, DC // P
KC, MC = 2, 4
RING = 4
LEAD = 3
WC = MC * P
ALPHA = 2.0 ** 0.25
LN_EPS = 1e-5
NORMS = 3
LAMBDA_INIT = 0.8 - 0.6
SCALE = HD ** -0.5
NEG = -1e30
ROT = 8
SLOTS = PAGES + 1
PT = 2
QUARTERS = 4


class Count:

    def __init__(self, n=0):
        self.n, self.term = n, 0

    def __call__(self, ahead=0):
        return self.term + (self.n + ahead)

    def add(self, by=1):
        self.n += by
        return self()


@contextmanager
def loop(eng, times, *steps):
    with eng.Fori(0, times) as i:
        starts = [c.n for c, _ in steps]
        for c, s in steps:
            c.term = i * s
        yield i
        for (c, s), n in zip(steps, starts):
            assert c.n == n + s, (c.n, n, s)
    for (c, s), n in zip(steps, starts):
        c.term, c.n = 0, n + times * s


class Progress:

    def __init__(self):
        self.split = Count()
        self.landed = [Count() for _ in range(RING)]
        self.tiles = Count()
        self.chunks = Count(RING)
        self.out = [Count(MC), Count(MC)]

    def steps(self, chunks):
        return ((self.split, 2 * chunks), *((slot, 16 * 2 * chunks // RING) for slot in self.landed),
                (self.tiles, 2 * (MC - 1)), (self.chunks, 2 * chunks), (self.out[0], MC), (self.out[1], MC))

    def skip_panel(self, banks, chunks):
        self.tiles.add(MC - 1)
        self.chunks.add(chunks)
        self.out[banks].add(MC)


def program(nc, a, out):
    with ExitStack() as ctx:
        def sem(name):
            return ctx.enter_context(nc.semaphore(name))

        top = nc.sbuf_base
        end = nc.sbuf_usable_end

        def at(name, shape, dt=F32, offset=None):
            nonlocal top
            size = int(np.prod(shape[1:])) * 4
            if offset is None:
                top = -(-top // 32) * 32
                offset, top = top, top + size
            assert offset + size <= end, (name, offset, size, end)
            return nc.alloc_sbuf_tensor_at(name, shape, dt, offset=offset)

        TILE = N * 4
        x_at = (top + 31) // 32 * 32
        x_hi = at("x_hi", [P, DT, N], F32R)
        x_lo = at("x_lo", [P, DT, N], F32R)
        y = at("y", [P, DT, N], F32, x_at)
        y_norm = at("y_norm", [P, DT, N], F32, x_at + DT * TILE)
        w_raw = at("w_raw", [P, RING, KC, WC])
        w_hi = at("w_hi", [P, RING, KC, WC], F32R)
        w_lo = at("w_lo", [P, RING, KC, WC], F32R)
        ident = at("ident", [P, P])
        ones = at("ones", [P, P])
        mask = at("mask", [P, 3, P])
        ln_g = at("ln_g", [P, 3, DT])
        ln_b = at("ln_b", [P, 3, DT])
        conv_w = at("conv_w", [P, 3, AT])
        conv_state = at("conv_state", [P, AT, B, 2])
        rope_cs = at("rope_cs", [P, 2, 3, ROT])
        subln = at("subln", [P, 1])
        lam_in = at("lam_in", [HD, 4])
        lam_prod = at("lam_prod", [HD, 2])
        lam = at("lam", [P, 4])
        page_ids = at("page_ids", [1, B * PAGES], I32)
        neg_eye = at("neg_eye", [B, B])
        ln_at = (top + 31) // 32 * 32
        one_sum = at("one_sum", [P, N])
        sq_sum = at("sq_sum", [P, N])
        shift = at("shift", [P, N])
        mean = at("mean", [P, N])
        mean_sq = at("mean_sq", [P, N])
        rstd = at("rstd", [P, N])
        eps = at("eps", [P, 2])
        warm = at("warm", [P, 1])
        area = (top + 31) // 32 * 32

        h_hi = at("h_hi", [P, FT, N], F32R, area)
        h_lo = at("h_lo", [P, FT, N], F32R, area + FT * TILE)
        hid = at("hid", [P, MC, N], F32, area + 2 * FT * TILE)

        top = area
        o_all = at("o_all", [P, HEADS, N])
        scores = at("scores", [P, B, SLOTS, 2 * HEADS])
        k_ring = at("k_ring", [P, 2, DC])
        qb_at = (top + 31) // 32 * 32
        q_bcast = at("q_bcast", [P, B, DC])
        m_hi = at("m_hi", [P, DT, N], F32R, qb_at)
        m_lo = at("m_lo", [P, DT, N], F32R, qb_at + DT * TILE)
        v_s = at("v_s", [B, DC])
        assert 2 * DT * TILE <= (B + 1) * DC * 4
        early = (top + 31) // 32 * 32
        z_q = at("z_q", [P, AT, N])
        z_k = at("z_k", [P, AT, N])
        v_tok = at("v_tok", [P, PT, DC])
        z_v = at("z_v", [P, AT, N])
        zv_at = early + 2 * AT * TILE + PT * DC * 4
        prob = at("prob", [P, 2, 3, P], F32, zv_at)
        attn = at("attn", [P, 3, P], F32, zv_at + 3072)
        attn_t = at("attn_t", [P, 3, P], F32, zv_at + 4608)
        top = early
        sig = at("sig", [P, 2, DT, N])
        assert zv_at + AT * TILE <= top
        c_at = top
        z_c = at("z_c", [P, 3, AT, N])
        q_s = at("q_s", [B, DC], F32, c_at)
        rope_t = at("rope_t", [P, 4, PT, 2 * HEADS, ROT], F32, c_at + 4096)
        qk_tok = at("qk_tok", [P, 3, DC], F32, c_at + AT * TILE)
        k_slots = [k_ring[:, 0], k_ring[:, 1], qk_tok[:, 0], qk_tok[:, 1]]
        stats = at("stats", [P, 16])
        s_tmp = at("s_tmp", [B, 2, 2 * HEADS])
        u = z_c[:, 2]
        conv_o = z_c[:, 1]
        conv_t = at("conv_t", [P, 3, AT, B], F32, ln_at)
        conv_new = at("conv_new", [P, AT, B, 2], F32, ln_at + 768)
        o_sqp = at("o_sqp", [P, 2, T], F32, ln_at + 1280)
        yc_hi = at("yc_hi", [P, AT, N], F32R, c_at)
        yc_lo = at("yc_lo", [P, AT, N], F32R, c_at + 2 * AT * TILE)
        o_hi = at("o_hi", [P, AT, N], F32R, c_at)
        o_lo = at("o_lo", [P, AT, N], F32R, c_at + AT * TILE)
        kr_at = qb_at - 2 * DC * 4
        s_max = at("s_max", [P, P], F32, kr_at)
        s_diag = at("s_diag", [P, P], F32, kr_at + 512)
        s_rec = at("s_rec", [P, P], F32, kr_at + 1024)
        s_attn = at("s_attn", [P, B, SLOTS, HEADS], F32, kr_at + 1536)
        s_attn2 = at("s_attn2", [P, B, SLOTS, HEADS], F32, kr_at + 4096)
        s_col = at("s_col", [P, 1], F32, kr_at + 7168)
        s_weights = at("s_weights", [P, B, PAGES, 2, HEADS], F32R, qb_at)
        s_sums = at("s_sums", [2 * HEADS, DC], F32, qb_at + 4096)
        o_sqs = at("o_sqs", [P, HEADS * B], F32, qb_at + 8192 + 32)
        own_head = at("own_head", [2 * HEADS, HEADS], F32, qb_at + 8192)

        ps = ctx.enter_context(nc.psum_tensor("ps", [P, 8, 512], F32))

        const_in = sem("const_in")
        page_ids_in = sem("page_ids_in")
        x_in = [sem(f"x_in{i}") for i in range(QUARTERS)]
        xs_in = sem("xs_in")
        made = sem("made")
        w_landed = [sem(f"w_landed{i}") for i in range(RING)]
        w_hi_ready = sem("w_hi_ready")
        w_lo_ready = sem("w_lo_ready")
        w_used = sem("w_used")
        tile_done = sem("tile_done")
        out_of = [sem("out_of_banks0"), sem("out_of_banks1")]
        x_hi_ready = sem("x_hi_ready")
        x_ready = sem("x_ready")
        h_hi_ready = sem("h_hi_ready")
        h_ready = sem("h_ready")
        pool_step = sem("pool_step")
        dve_step = sem("dve_step")
        lam_prod_ready = sem("lam_prod_ready")
        lam_sum = sem("lam_sum")
        lam_exp = sem("lam_exp")
        ln_first = sem("ln_first")
        ln_first_sum = sem("ln_first_sum")
        ln_shifted = sem("ln_shifted")
        ln_squared = sem("ln_squared")
        ln_partial = sem("ln_partial")
        ln_pairs = sem("ln_pairs")
        ln_sums = sem("ln_sums")
        ln_var = sem("ln_var")
        ln_std = sem("ln_std")
        ln_scaled = sem("ln_scaled")
        ln_out = sem("ln_out")
        turned = sem("turned")
        tok_ready = sem("tok_ready")
        roped = sem("roped")
        q_kept = sem("q_kept")
        back = sem("back")
        back_ready = sem("back_ready")
        new_scored = sem("new_scored")
        q_stored = sem("q_stored")
        qb_landed = sem("qb_landed")
        k_landed = [sem(f"k_landed{i}") for i in range(4)]
        k_mult = sem("k_mult")
        k_free = sem("k_free")
        sc_done = sem("sc_done")
        sc_masked = sem("sc_masked")
        sc_max = sem("sc_max")
        sc_exp = sem("sc_exp")
        at_ready = sem("at_ready")
        at_turned = sem("at_turned")
        att_ready = sem("att_ready")
        pv_done = sem("pv_done")
        o_ready = sem("o_ready")
        conv_done = sem("conv_done")
        conv_new_ready = sem("conv_new_ready")
        conv_hi = sem("conv_hi")
        yc_ready = sem("yc_ready")
        ss_max1 = sem("ss_max1")
        ss_turned = sem("ss_turned")
        ss_diag = sem("ss_diag")
        ss_bcast = sem("ss_bcast")
        ss_shift = sem("ss_shift")
        ss_exp = sem("ss_exp")
        ss_sums = sem("ss_sums")
        ss_den = sem("ss_den")
        ss_rec = sem("ss_rec")
        ss_attn = sem("ss_attn")
        pv_weights_hi = sem("pv_weights_hi")
        pv_weights = sem("pv_weights")
        seq_out = sem("seq_out")
        seq_turned = sem("seq_turned")
        seqs_out = sem("seqs_out")
        o_square = sem("o_square")
        o_normed = sem("o_normed")
        o_sumsq = sem("o_sumsq")
        o_std = sem("o_std")
        o_scaled = sem("o_scaled")
        o_hi_ready = sem("o_hi_ready")
        o_split = sem("o_split")
        m_sum = sem("m_sum")
        m_hi_ready = sem("m_hi_ready")
        m_ready = sem("m_ready")
        kv_stored = sem("kv_stored")
        conv_stored = sem("conv_stored")
        y_stored = sem("y_stored")

        q_scratch = nc.dram_tensor("q_scratch", [B, DC], F32, kind="Internal").ap()
        block = ctx.enter_context(nc.Block())

        K_CH, H_CH, A_CH = DT // KC, FT // KC, AT // KC
        FFN_PAIRS = F // WC
        OUT_PAIRS = D // WC // 2
        C_PAIRS = 3 * DC // (2 * WC)
        G_PAIRS = 2 * D // (2 * WC)
        CONSTS, MADE = 16 * 7, 8
        NORM_AFTER = 3, 6
        V_TURN, K_BACK, FIRST_HEAD, HEAD_CH = 1, 5, 7, 5

        VALUE_PANELS = [K_CH, K_CH, A_CH, A_CH]
        PAGES_AFTER = {K_CH: (3, 3, 2, 2, 2, 2, 2, 0), A_CH: (6, 5, 5, 0)}
        TURN_EVEN = {K_CH: 3, A_CH: 2}

        def through_page(chunks, k):
            c = next(c for c in range(chunks) if sum(PAGES_AFTER[chunks][:c + 1]) >= k)
            return c + 1 + k

        def sums_bank(b):
            return 4 * (1 - b // 2 % 2) + (2 if b % 2 == 0 else 0)

        HEAD_NORM = 3

        def at_head(h):
            return FIRST_HEAD + HEAD_CH * h

        assert at_head(HEADS) <= 2 * C_PAIRS * K_CH - 1
        assert KC * WC == DC and 2 * len(VALUE_PANELS) == B

        @block.sync
        def _(sp):
            n = Count()
            pages = Count()

            def chunk(w, k0, col):
                sp.wait_ge(w_lo_ready, n.add())
                s = (n.n - 1) % RING
                src = w[k0 * P:(k0 + KC) * P, bass.ds(col, WC)].rearrange("(k p) n -> p k n", p=P)
                sp.dma_start(w_raw[:, s], src).then_inc(w_landed[s], 16)

            def ffn(gate, up, down):
                with loop(sp, FFN_PAIRS, (n, 2 * K_CH)) as i:
                    for w in (gate, up):
                        for c in range(K_CH):
                            chunk(w, KC * c, i * WC)
                out_proj(down, H_CH)

            def out_pair(w, chunks, i, part=slice(None)):
                for p, c in [(p, c) for p in range(2) for c in range(chunks)][part]:
                    chunk(w, KC * c, i * (2 * WC) + p * WC)

            def out_proj(w, chunks):
                with loop(sp, OUT_PAIRS, (n, 2 * chunks)) as i:
                    out_pair(w, chunks, i)

            def page_numbers(seq):
                return nc.values_load_multi_w_load_instructions(
                    page_ids[0:1, bass.ds(seq * PAGES, PAGES)], engines=[mybir.EngineType.SP],
                    min_val=0, max_val=a["cache_k"].shape[1] - 1)[1]

            def page(cache, p, dst):
                return sp.dma_start(dst, cache[0, bass.ds(p, 1)].rearrange("a k h e -> (a k) (h e)"))

            def w_in_panel(i, p, after=None):
                for c in range(K_CH):
                    chunk(a["w_in"][0], KC * c, i * (2 * WC) + p * WC)
                    if after is not None:
                        after(c)

            def k_page(seq_ids, j, slot, free):
                sp.wait_ge(k_free, free)
                page(a["cache_k"], seq_ids[j], k_slots[slot]).then_inc(k_landed[slot], 16)

            def w_in_pair(i, seq):
                ids = page_numbers(seq)
                for p in range(2):
                    def keys(c):
                        if c % 2 == 1:
                            j = (p * K_CH + c) // 2
                            k_page(ids, j, j % 2, pages.add())
                    w_in_panel(i, p, keys)

            ffn(a["ffn1_w_gate"][0], a["ffn1_w_up"][0], a["ffn1_w_down"][0])
            for i in range(2):
                for p in range(2):
                    w_in_panel(i, p)
            sp.wait_ge(page_ids_in, 16)
            sp.wait_ge(back, 1)
            seq_ids = []

            def keys(c):
                if c == 0:
                    return
                for j in (c - 1,) if c < 2 * K_CH - 1 else (c - 1, c):
                    if j % PAGES == 0:
                        seq_ids[:] = page_numbers(j // PAGES)
                    pages.add()
                    k_page(seq_ids, j % PAGES, j % 4, max(j - 1, 1))
            for p in range(2):
                w_in_panel(2, p, lambda c: keys(p * K_CH + c))
            with loop(sp, B - 2, (n, 2 * K_CH), (pages, PAGES)) as i:
                w_in_pair(i + 3, i + 2)

            def v_page(number):
                sp.wait_ge(w_lo_ready, n.add())
                s = (n.n - 1) % RING
                page(a["cache_v"], number, w_raw[:, s].rearrange("p k n -> p (k n)")).then_inc(w_landed[s], 16)

            out_pair(a["w_conv_out"][0], A_CH, 0)
            for p, chunks in enumerate(VALUE_PANELS):
                ids = []
                for c in range(chunks):
                    if chunks == K_CH:
                        chunk(a["w_in"][0], KC * c, (2 + C_PAIRS + G_PAIRS) * (2 * WC) + p * WC)
                    else:
                        chunk(a["w_conv_out"][0], KC * c, 2 * WC + (p - 2) * WC)
                    done = sum(PAGES_AFTER[chunks][:c])
                    for k in range(done, done + PAGES_AFTER[chunks][c]):
                        if k % PAGES == 0:
                            ids = page_numbers(2 * p + k // PAGES)
                        v_page(ids[k % PAGES])
            out_proj(a["w_attn_out"][0], A_CH)
            out_proj(a["w_o"][0], K_CH)
            ffn(a["ffn2_w_gate"][0], a["ffn2_w_up"][0], a["ffn2_w_down"][0])
            y_out = out["y_t"].rearrange("(t p) n -> p t n", p=P)
            for i in range(0, DT, MC):
                sp.wait_ge(ln_out, 2 * DT // KC + (i + MC) // KC)
                sp.dma_start(y_out[:, i:i + MC], y_norm[:, i:i + MC]).then_inc(y_stored, 16)
            sp.wait_ge(y_stored, 16 * DT // MC)
            sp.wait_ge(kv_stored, 16 * 4)
            sp.wait_ge(conv_stored, 16 * 2)

        def low_part(engine, queue, k, i, step, steps):
            two = slice(KC * i, KC * (i + 1))
            queue.wait_ge(ln_out, (k - 1) * DT // KC + i + 1)
            for t in range(KC * i, KC * (i + 1)):
                ins = engine.tensor_scalar(y_norm[:, t], y_norm[:, t], ln_g[:, k - 1, t:t + 1], ln_b[:, k - 1, t:t + 1],
                                           ALU.mult, ALU.add)
            ins.then_inc(step, 1)
            queue.wait_ge(step, steps.add())
            engine.tensor_tensor(x_lo[:, two], y_norm[:, two], x_hi[:, two].bitcast(F32), ALU.subtract).then_inc(x_ready, 1)

        @block.gpsimd
        def _(pool):
            nc.gpsimd.memset(ones[:], 1.0).then_inc(made, 1)
            nc.gpsimd.memset(ident[:], 0.0).then_inc(made, 1)
            nc.gpsimd.memset(mask[:], 0.0).then_inc(made, 1)
            nc.gpsimd.memset(eps[:, 0:1], LN_EPS / ALPHA ** 2).then_inc(made, 1)
            nc.gpsimd.memset(eps[:, 1:2], LN_EPS).then_inc(made, 1)
            pool.wait_ge(made, 5)
            nc.gpsimd.affine_select(out=ident[:], in_=ident[:], compare_op=ALU.not_equal, fill=1.0, base=0,
                                    pattern=[[-1, P]], channel_multiplier=1).then_inc(made, 1)
            for j in (0, 2):
                nc.gpsimd.affine_select(out=mask[:, j], in_=mask[:, j], compare_op=ALU.is_ge, fill=NEG, base=0,
                                        pattern=[[-1, P]], channel_multiplier=1).then_inc(made, 1)
            pool.dma_start(page_ids[:], a["page_table"]).then_inc(page_ids_in, 16)
            for dst, src in ((ln_g, "ln_g"), (ln_b, "ln_b"), (conv_w, "conv_w"), (conv_state, "state_conv"),
                             (rope_cs, "rope"), (subln, "subln_g"), (lam_in, "lambdas")):
                pool.dma_start(dst[:], a[src]).then_inc(const_in, 16)
            steps = Count()
            pool.wait_ge(x_ready, DT // KC + 1)
            for i in range(1, DT // KC):
                low_part(nc.gpsimd, pool, 1, i, pool_step, steps)
            pool.wait_ge(q_kept, 1)
            pool.dma_start(q_scratch, q_s[:]).then_inc(q_stored, 16)
            pool.wait_ge(q_stored, 16)
            for b in range(B):
                pool.dma_start(q_bcast[:, b], q_scratch[b:b + 1].broadcast_to([P, DC])).then_inc(qb_landed, 16)
            pool.wait_ge(qb_landed, 16 * B)
            for page in range(B * PAGES):
                if page < 2 * PAGES:
                    slot, uses = page % 4, page // 4 + 1
                else:
                    slot, uses = page % 2, 2 * PAGES // 4 + (page - 2 * PAGES) // 2 + 1
                pool.wait_ge(k_landed[slot], 16 * uses)
                keys = k_slots[slot]
                nc.gpsimd.tensor_tensor(keys, keys, q_bcast[:, page // PAGES], ALU.mult).then_inc(k_mult, 1)
            pool.wait_ge(x_ready, 2 * DT // KC + 1)
            for i in range(1, DT // KC):
                low_part(nc.gpsimd, pool, 2, i, pool_step, steps)

        @block.tensor
        def _(pe):
            n = Count()
            uses = [Count(), Count()]

            def panel(banks, hi, lo, chunks, after=None, ready=None, last_bank=None):
                for c in range(chunks):
                    if after is not None and c > 0:
                        after(c - 1)
                    pe.wait_ge(w_lo_ready, n.add() + RING)
                    s = (n.n - 1) % RING
                    if ready is not None:
                        pe.wait_ge(*ready(c))
                    for m in range(MC):
                        acc = ps[:, 4 * banks + m, 0:N]
                        if c == 0:
                            pe.wait_ge(out_of[banks], uses[banks].add())
                            if last_bank is not None and m == MC - 1:
                                pe.wait_ge(*last_bank)
                        for k in range(KC):
                            kt = c * KC + k
                            wh, wl = w_hi[:, s, k, m * P:(m + 1) * P], w_lo[:, s, k, m * P:(m + 1) * P]
                            nc.tensor.matmul(acc, wh, hi[:, kt], start=(kt == 0), stop=False)
                            nc.tensor.matmul(acc, wh, lo[:, kt], start=False, stop=False)
                            mm = nc.tensor.matmul(acc, wl, hi[:, kt], start=False, stop=(kt == chunks * KC - 1))
                        if m == MC - 1:
                            mm.then_inc(w_used, 1)
                        elif c == chunks - 1:
                            mm.then_inc(tile_done, 1)
                if after is not None:
                    after(chunks - 1)

            def pairs(times, hi, lo, chunks, ready=None):
                with loop(pe, times, (n, 2 * chunks), (uses[0], MC), (uses[1], MC)):
                    for banks in range(2):
                        panel(banks, hi, lo, chunks, ready=ready if banks == 0 else None)

            def x_split(base):
                return lambda c: (x_ready, base + c + 1)

            def pair(hi, lo, chunks, ready=None):
                for banks in range(2):
                    panel(banks, hi, lo, chunks, ready=ready if banks == 0 else None)

            def ffn(k, ready, norm):
                pairs(FFN_PAIRS, x_hi, x_lo, K_CH, x_split(ready))
                done = 1 + FFN_PAIRS * (k - 1)
                out_and_norm(norm, h_hi, h_lo, H_CH, ready=lambda c: (h_ready, done + c * KC // MC + 1))

            def banks_free():
                for banks in range(2):
                    pe.wait_ge(out_of[banks], uses[banks](MC))

            def all_features(bank, x, start, stop):
                return nc.tensor.matmul(ps[:, bank, 0:N], ones[:], x, start=start, stop=stop)

            def out_and_norm(k, hi, lo, chunks, ready=None):
                pairs(OUT_PAIRS - 1, hi, lo, chunks, ready)

                def first_tiles(c):
                    if c == NORM_AFTER[0]:
                        pe.wait_ge(ln_first, k)
                        all_features(4, one_sum[:], True, True).then_inc(ln_first_sum, 1)

                def most_tiles(c):
                    if c == NORM_AFTER[1]:
                        pe.wait_ge(ln_partial, k)
                        all_features(0, one_sum[:], True, False)
                        all_features(1, sq_sum[:], True, False)

                panel(0, hi, lo, chunks, after=first_tiles)
                panel(1, hi, lo, chunks, after=most_tiles)
                pe.wait_ge(ln_pairs, 4 * k - 3)
                all_features(0, mean[:], False, False)
                pe.wait_ge(ln_pairs, 4 * k - 2)
                all_features(1, y_norm[:, DT - 4], False, False)
                pe.wait_ge(ln_pairs, 4 * k - 1)
                all_features(0, mean_sq[:], False, True).then_inc(ln_sums, 1)
                pe.wait_ge(ln_pairs, 4 * k)
                all_features(1, y_norm[:, DT - 2], False, True).then_inc(ln_sums, 1)

            def to_tokens(z, j):
                w = P if j < PT else B
                bank = 4 + 2 * j if j < PT else (0 if z is z_v else 2)
                for t in range(AT):
                    mm = nc.tensor.transpose(ps[0:w, bank + t // 4, (t % 4) * P:(t % 4 + 1) * P],
                                             z[:, t, j * P:j * P + w], ident[:])
                mm.then_inc(turned, 1)

            def from_tokens():
                for h in range(HEADS):
                    for j in range(PT):
                        mm = nc.tensor.transpose(ps[:, 4 + h // 2, (h % 2) * T + j * P:(h % 2) * T + (j + 1) * P],
                                                 qk_tok[:, j, h * VD:(h + 1) * VD], ident[:])
                mm.then_inc(back, 1)

            pe.sem_inc(w_used, RING)
            for banks in range(2):
                pe.sem_inc(out_of[banks], MC)
            pe.wait_ge(made, MADE)
            ffn(1, 0, 1)
            pair(x_hi, x_lo, K_CH, ready=x_split(DT // KC))
            banks_free()
            for j in (2, 0, 1):
                to_tokens(z_q, j)
            pe.wait_ge(tok_ready, 1)

            def q_back(c):
                if c == 3:
                    pe.wait_ge(roped, 1)
                    from_tokens()
                if c == 5:
                    pe.wait_ge(back_ready, 1)
                    pe.wait_ge(lam_prod_ready, 2)
                    nc.tensor.matmul(ps[:, 7, 0:2], ones[0:HD, :], lam_prod[:], start=True, stop=True).then_inc(lam_sum, 1)

            panel(0, x_hi, x_lo, K_CH, after=q_back)
            pe.wait_ge(lam_exp, 1)
            panel(1, x_hi, x_lo, K_CH)
            pair(x_hi, x_lo, K_CH)
            banks_free()
            to_tokens(z_k, 2)
            to_tokens(z_v, 2)
            to_tokens(z_k, 0)
            to_tokens(z_k, 1)
            pe.wait_ge(tok_ready, 5)

            def prompt_scores(h):
                if h == 0:
                    pe.wait_ge(back_ready, 2)
                else:
                    pe.wait_ge(sc_masked, 2 * h)
                for c in range(2):
                    q, k = z_q[c * HD:(c + 1) * HD, h], z_k[c * HD:(c + 1) * HD, h]
                    nc.tensor.matmul(ps[:, 4 + c, 0:P], q[:, 0:P], k[:, 0:P], start=True, stop=True)
                    mm = nc.tensor.matmul(ps[:, 4 + c, P:3 * P], q[:, P:T], k[:, 0:T], start=True, stop=True)
                mm.then_inc(sc_done, 1)

            def turn_attention(h):
                pe.wait_ge(at_ready, h + 1)
                if h >= 1:
                    pe.wait_ge(att_ready, h)
                for b in range(3):
                    mm = nc.tensor.transpose(ps[:, 6, b * P:(b + 1) * P], attn[:, b], ident[:])
                mm.then_inc(at_turned, 1)

            def prompt_values(h):
                pe.wait_ge(att_ready, h + 1)
                if h >= 1:
                    pe.wait_ge(o_ready, h)
                v = v_tok[:, :, h * VD:(h + 1) * VD]
                nc.tensor.matmul(ps[:, 7, 0:P], v[:, 0], attn_t[:, 0], start=True, stop=True)
                nc.tensor.matmul(ps[:, 7, P:T], v[:, 0], attn_t[:, 1], start=True, stop=False)
                nc.tensor.matmul(ps[:, 7, P:T], v[:, 1], attn_t[:, 2], start=False, stop=True).then_inc(pv_done, 1)

            for p in range(2 * C_PAIRS):
                def attention(c):
                    x = p * K_CH + c
                    if x == V_TURN:
                        pe.wait_ge(tok_ready, 7)
                        to_tokens(z_v, 0)
                        to_tokens(z_v, 1)
                    if x == K_BACK:
                        pe.wait_ge(tok_ready, 9)
                        pe.wait_ge(roped, 2)
                        from_tokens()
                    for h in range(HEADS):
                        if x == at_head(h) + HEAD_CH:
                            prompt_values(h)
                        if x == at_head(h) + HEAD_CH - 1:
                            turn_attention(h)
                        if x == at_head(h):
                            prompt_scores(h)

                panel(0, x_hi, x_lo, K_CH, after=attention)
            pe.wait_ge(o_ready, HEADS)
            with loop(pe, G_PAIRS - 1, (n, 2 * K_CH), (uses[0], MC), (uses[1], MC)) as i:
                def head_squares(c):
                    if c == HEAD_NORM:
                        pe.wait_ge(out_of[1], uses[1](MC))
                        pe.wait_ge(o_square, i + 1)
                        nc.tensor.matmul(ps[:, 4], ones[:], o_sqp[:].rearrange("p h n -> p (h n)"),
                                         start=True, stop=True).then_inc(o_sumsq, 1)

                panel(0, x_hi, x_lo, K_CH, after=head_squares)
                pe.wait_ge(o_std, i + 1)
                panel(1, x_hi, x_lo, K_CH)
            pe.wait_ge(yc_ready, 1)
            def softmax(c):
                if c == 1:
                    pe.wait_ge(out_of[1], uses[1](MC))
                    pe.wait_ge(ss_max1, 1)
                    nc.tensor.transpose(ps[:, 7, 0:P], s_max[:], ident[:]).then_inc(ss_turned, 1)
                if c == A_CH - 1:
                    pe.wait_ge(ss_diag, 1)
                    nc.tensor.matmul(ps[:, 7, 0:P], ones[:], s_diag[:], start=True, stop=True).then_inc(ss_bcast, 1)

            def softmax_sums(c):
                if c == 1:
                    pe.wait_ge(out_of[0], uses[0](MC))
                    pe.wait_ge(ss_sums, 1)
                    nc.tensor.matmul(ps[:, 0, 0:P], ones[:], s_max[:], start=True, stop=True).then_inc(ss_den, 1)

            panel(0, yc_hi, yc_lo, A_CH, after=softmax)
            panel(1, yc_hi, yc_lo, A_CH, after=softmax_sums, last_bank=(ss_shift, 1))
            pe.wait_ge(ss_rec, 1)

            def by_head(b, seqs=1):
                place = ps[:, 7 - 4 * (b // 2 % 2), b * HEADS:(b + seqs) * HEADS]
                return place.rearrange("p (b h) -> p b h", b=seqs)

            def page_values(b, j):
                pe.wait_ge(w_lo_ready, n.add() + RING)
                s = (n.n - 1) % RING
                bank = sums_bank(b)
                for w in (w_hi, w_lo):
                    for c in range(KC):
                        mm = nc.tensor.matmul(ps[0:2 * HEADS, bank + c], s_weights[:, b, j].rearrange("p c h -> p (c h)"),
                                              w[:, s, c], start=(j == 0 and w is w_hi), stop=(j == PAGES - 1 and w is w_lo))
                mm.then_inc(w_used, 1)

            def turn_seq(b):
                pe.wait_ge(seq_out, b + 1)
                if b % 2 == 0:
                    for h in range(HEADS):
                        nc.tensor.matmul(by_head(b, 2)[:, :, h], v_s[:, h * VD:(h + 1) * VD],
                                         s_attn[0:B, b:b + 2, PAGES, h],
                                         start=(h == 0), stop=False, skip_group_check=True)
                for h in range(HEADS):
                    mm = nc.tensor.matmul(by_head(b)[:, 0, h:h + 1], s_sums[:, h * VD:(h + 1) * VD], own_head[:, h:h + 1],
                                          start=False, stop=True, skip_group_check=True)
                mm.then_inc(seq_turned, 1)

            for p, chunks in enumerate(VALUE_PANELS):
                def pages(c):
                    if c == 0:
                        pe.wait_ge(pv_weights, 1)
                        rest = 1 - p % 2
                        pe.wait_ge(out_of[rest], uses[rest](MC))
                    if c == TURN_EVEN[chunks]:
                        turn_seq(2 * p)
                    if p == 0 and c == HEAD_NORM:
                        pe.wait_ge(o_square, G_PAIRS)
                        nc.tensor.matmul(ps[:, 6], ones[:], o_sqp[:].rearrange("p h n -> p (h n)"),
                                         start=True, stop=True).then_inc(o_sumsq, 1)
                    done = sum(PAGES_AFTER[chunks][:c])
                    for k in range(done, done + PAGES_AFTER[chunks][c]):
                        page_values(2 * p + k // PAGES, k % PAGES)

                hi, lo = (x_hi, x_lo) if chunks == K_CH else (yc_hi, yc_lo)
                panel(p % 2, hi, lo, chunks, after=pages, last_bank=(seqs_out, p) if p > 0 else None)
                turn_seq(2 * p + 1)
                if p == 0:
                    pe.wait_ge(o_std, G_PAIRS)
            pe.wait_ge(o_square, G_PAIRS + 1)
            nc.tensor.matmul(ps[:, 0, 0:B * HEADS], ones[:], o_sqs[:], start=True, stop=True).then_inc(o_sumsq, 1)
            pe.wait_ge(o_std, G_PAIRS + 1)
            pairs(OUT_PAIRS, o_hi, o_lo, A_CH, ready=lambda c: (o_split, c + 1))
            out_and_norm(2, m_hi, m_lo, K_CH, ready=lambda c: (m_ready, c * KC // MC + 1))
            ffn(2, 2 * DT // KC, 3)

        @block.scalar
        def _(sc):
            at_ = Progress()
            n, out_n = at_.split, at_.out
            panels_h = Count()

            def split_hi(times):
                for _ in range(times):
                    s = n.n % RING
                    sc.wait_ge(w_used, n(1))
                    sc.wait_ge(w_landed[s], at_.landed[s].add(16))
                    n.add()
                    nc.scalar.activation(w_hi[:, s], w_raw[:, s], ACT.Copy).then_inc(w_hi_ready, 1)

            def take_out(banks, chunks, func, dst):
                at_.chunks.add(chunks)
                for m in range(MC):
                    if m < MC - 1:
                        sc.wait_ge(tile_done, at_.tiles.add())
                    else:
                        sc.wait_ge(w_used, at_.chunks())
                    nc.scalar.activation(dst(m), ps[:, 4 * banks + m, 0:N], func).then_inc(out_of[banks], 1)
                    out_n[banks].add()

            def ffn(norm):
                with loop(sc, FFN_PAIRS, *at_.steps(K_CH), (panels_h, 1)) as i:
                    split_hi(K_CH - 1)
                    sc.wait_ge(h_ready, panels_h(1))
                    take_out(0, K_CH, ACT.Silu, lambda m: hid[:, m])
                    split_hi(K_CH + 1)
                    at_.skip_panel(1, K_CH)
                    sc.wait_ge(out_of[1], out_n[1]())
                    nc.scalar.activation(h_hi[:, bass.ds(i * MC, MC)], hid[:], ACT.Copy).then_inc(h_hi_ready, 1)
                    panels_h.add()
                out_and_norm(norm, H_CH)

            def only_split(times, chunks):
                with loop(sc, times, *at_.steps(chunks)):
                    split_hi(2 * chunks)
                    at_.skip_panel(0, chunks)
                    at_.skip_panel(1, chunks)

            def square(tiles):
                nc.scalar.activation(y_norm[:, tiles], y[:, tiles], ACT.Square).then_inc(ln_squared, 1)

            def out_and_norm(k, chunks):
                only_split(OUT_PAIRS - 1, chunks)
                ends = [chunks, chunks - (LEAD if k == NORMS else 0)]
                split_hi(2 * LEAD)
                sc.wait_ge(ln_shifted, 2 * k - 1)
                square(slice(0, 2 * MC))
                nc.scalar.activation(warm[:], eps[:, 1:2], ACT.Sqrt)
                split_hi(ends[0] - 2 * LEAD + 2)
                sc.wait_ge(ln_shifted, 2 * k)
                square(slice(2 * MC, 3 * MC))
                split_hi(ends[1] - 2)
                at_.skip_panel(0, chunks)
                at_.skip_panel(1, chunks)
                for m in range(MC):
                    sc.wait_ge(out_of[1], out_n[1](m + 1 - MC))
                    square(slice(DT - MC + m, DT - MC + m + 1))
                sc.wait_ge(ln_var, k)
                nc.scalar.activation(rstd[:], mean_sq[:], ACT.Sqrt, bias=eps[:, 0:1]).then_inc(ln_std, 1)
                for i in range(DT // KC):
                    sc.wait_ge(ln_scaled, (k - 1) * DT // KC + i + 1)
                    for t in range(KC * i, KC * (i + 1)):
                        g, b = ln_g[:, k - 1, t:t + 1], ln_b[:, k - 1, t:t + 1]
                        dst = x_hi if k < NORMS else y_norm
                        ins = nc.scalar.activation(dst[:, t], y_norm[:, t], ACT.Identity, bias=b, scale=g)
                    ins.then_inc(ln_out, 1)

            def z_pair(tile, func=ACT.Copy):
                for banks in range(2):
                    split_hi(K_CH)
                    take_out(banks, K_CH, func, lambda m: tile(MC * banks + m))

            def tokens(dst, j, bank):
                k = tokens.n = tokens.n + 1
                sc.wait_ge(turned, k)
                w = P if j < PT else B
                nc.scalar.activation(dst, ps[0:w, bank:bank + 2].rearrange("p b n -> p (b n)"), ACT.Copy).then_inc(tok_ready, 1)
            tokens.n = 0

            def turned_back(k, z):
                sc.wait_ge(back, k)
                nc.scalar.activation(z[:, :, 0:T], ps[:, 4:8].rearrange("p b (h t) -> p (b h) t", h=2),
                                     ACT.Copy).then_inc(back_ready, 1)

            x_prompt = a["x_prompt_t"].rearrange("(t p) n -> p t n", p=P)
            quarters = [slice(i, i + DT // QUARTERS) for i in range(0, DT, DT // QUARTERS)]
            for i, q in enumerate(quarters):
                sc.dma_start(y_norm[:, q, 0:T], x_prompt[:, q]).then_inc(x_in[i], 16)
                if i == 0:
                    sc.dma_start(y_norm[:, :, T:N], a["x_sample_t"].rearrange("(t p) n -> p t n", p=P)).then_inc(xs_in, 16)
            sc.wait_ge(made, 5)
            nc.scalar.activation(warm[:], eps[:, 1:2], ACT.Silu)
            for i, q in enumerate(quarters):
                if i < LEAD:
                    split_hi(1)
                sc.wait_ge(x_in[i], 16)
                if i == 0:
                    sc.wait_ge(xs_in, 16)
                nc.scalar.activation(x_hi[:, q], y_norm[:, q], ACT.Copy).then_inc(x_hi_ready, 1)
            sc.wait_ge(made, MADE)
            sc.wait_ge(const_in, CONSTS)
            ffn(norm=1)
            z_pair(lambda m: z_q[:, m])
            tokens(qk_tok[0:B, 2], 2, 2)
            tokens(qk_tok[:, 0], 0, 4)
            tokens(qk_tok[:, 1], 1, 6)
            split_hi(4)
            turned_back(1, z_q)
            split_hi(2)
            sc.wait_ge(lam_sum, 1)
            nc.scalar.activation(lam[:, 0:2], ps[:, 7, 0:2], ACT.Exp).then_inc(lam_exp, 1)
            split_hi(K_CH - 6)
            take_out(0, K_CH, ACT.Copy, lambda m: z_k[:, m])
            split_hi(K_CH)
            take_out(1, K_CH, ACT.Copy, lambda m: z_k[:, MC + m])
            split_hi(K_CH)
            take_out(0, K_CH, ACT.Copy, lambda m: z_v[:, m])
            split_hi(K_CH - 1)
            take_out(1, K_CH, ACT.Copy, lambda m: z_v[:, MC + m])
            sc.wait_ge(q_kept, 1)
            tokens(qk_tok[0:B, 2], 2, 2)
            tokens(v_s[:], 2, 0)
            split_hi(1)
            sc.wait_ge(k_free, 2 + 2 * PAGES)
            tokens(qk_tok[:, 0], 0, 4)
            tokens(qk_tok[:, 1], 1, 6)

            def prompt_exp(h):
                sc.wait_ge(sc_max, h + 1)
                for c in range(2):
                    for j in range(2):
                        blocks = prob[:, c, 0:1] if j == 0 else prob[:, c, 1:3]
                        i = 2 * c + j
                        nc.scalar.activation(blocks, blocks, ACT.Exp, bias=stats[:, 4 + i:5 + i],
                                             accum_out=stats[:, 8 + i:9 + i]).then_inc(sc_exp, 1)

            def attention_turned(h):
                sc.wait_ge(at_turned, h + 1)
                if h >= 1:
                    sc.wait_ge(pv_done, h)
                nc.scalar.activation(attn_t[:], ps[:, 6, 0:3 * P].rearrange("p (b q) -> p b q", b=3),
                                     ACT.Copy).then_inc(att_ready, 1)

            def prompt_out(h):
                sc.wait_ge(pv_done, h + 1)
                nc.scalar.activation(o_all[:, h, 0:T], ps[:, 7, 0:T], ACT.Copy).then_inc(o_ready, 1)

            z_all = z_c[:].rearrange("p c t n -> p (c t) n")
            for x in range(LEAD, 2 * C_PAIRS * K_CH + LEAD):
                split_hi(1)
                if x == V_TURN + LEAD:
                    tokens(v_tok[:, 0], 0, 4)
                    tokens(v_tok[:, 1], 1, 6)
                if x == K_BACK + LEAD:
                    turned_back(2, z_k)
                    sc.wait_ge(tok_ready, 9)
                    for dst, src in (("k_prompt", qk_tok[:, 0:PT]), ("v_prompt", v_tok[:])):
                        sc.dma_start(out[dst].rearrange("(j p) e -> p j e", p=P), src).then_inc(kv_stored, 16)
                    for dst, src in (("k_sample", qk_tok[0:B, 2]), ("v_sample", v_s[:])):
                        sc.dma_start(out[dst], src).then_inc(kv_stored, 16)
                for h in range(HEADS):
                    if x == at_head(h) + HEAD_CH - 1 + LEAD:
                        attention_turned(h)
                    if x == at_head(h) + HEAD_CH + LEAD:
                        prompt_out(h)
                    if x == at_head(h) + RING + 1:
                        prompt_exp(h)
                p, last = divmod(x - LEAD, K_CH)
                if last == K_CH - 1:
                    if p == 0:
                        sc.wait_ge(new_scored, 1)
                    if p == 2:
                        sc.wait_ge(kv_stored, 16 * 4)
                    take_out(0, K_CH, ACT.Copy, lambda m: z_all[:, MC * p + m])
            sig_all = sig[:].rearrange("p c t n -> p (c t) n")

            def head_norm(i):
                nc.scalar.activation(o_sqp[:], o_all[:, bass.ds(i * 2, 2), 0:T], ACT.Square).then_inc(o_square, 1)
                split_hi(HEAD_NORM + 1)
                sc.wait_ge(o_sumsq, i + 1)
                nc.scalar.activation(o_sqp[:].rearrange("p h n -> p (h n)"), ps[:, 4], ACT.Sqrt,
                                     bias=eps[:, 1:2], scale=1.0 / VD).then_inc(o_std, 1)
                split_hi(K_CH - (HEAD_NORM + 1))

            sc.wait_ge(o_ready, HEADS)
            head_norm(0)
            take_out(0, K_CH, ACT.Sigmoid, lambda m: sig_all[:, m])
            sc.wait_ge(conv_new_ready, 3)
            sc.dma_start(out["conv_prompt_t"].rearrange("(t p) k -> p t k", p=P), u[:, :, T - 2:T]).then_inc(conv_stored, 16)
            sc.dma_start(out["conv_sample_t"].rearrange("(t p) b k -> p t b k", p=P), conv_new[:]).then_inc(conv_stored, 16)
            split_hi(K_CH)
            take_out(1, K_CH, ACT.Sigmoid, lambda m: sig_all[:, MC + m])
            sc.wait_ge(conv_done, 1)
            nc.scalar.activation(yc_hi[:], conv_o, ACT.Copy).then_inc(conv_hi, 1)
            with loop(sc, G_PAIRS - 2, *at_.steps(K_CH)) as i:
                sc.wait_ge(o_normed, i + 1)
                head_norm(i + 1)
                take_out(0, K_CH, ACT.Sigmoid, lambda m: sig_all[:, bass.ds(i * 8 + (8 + m), 1)])
                split_hi(K_CH)
                take_out(1, K_CH, ACT.Sigmoid, lambda m: sig_all[:, bass.ds(i * 8 + (8 + MC + m), 1)])
            split_hi(A_CH)
            sc.wait_ge(ss_shift, 1)
            nc.scalar.activation(scores[:], scores[:], ACT.Exp, scale=SCALE).then_inc(ss_exp, 1)
            sc.wait_ge(o_normed, G_PAIRS - 1)
            nc.scalar.activation(o_sqp[:], o_all[:, HEADS - 2:HEADS, 0:T], ACT.Square).then_inc(o_square, 1)
            split_hi(A_CH)
            sc.wait_ge(ss_attn, 1)
            nc.scalar.activation(s_weights[:, :, :, 0], s_attn[:, :, 0:PAGES], ACT.Copy).then_inc(pv_weights_hi, 1)
            for banks in range(2):
                at_.skip_panel(banks, A_CH)

            def sums_out(b):
                sc.wait_ge(w_used, at_.chunks(through_page(chunks, PAGES * (b % 2 + 1))))
                if b > 0:
                    sc.wait_ge(seq_turned, b)
                bank = sums_bank(b)
                nc.scalar.activation(s_sums[:], ps[0:2 * HEADS, bank:bank + KC].rearrange("p c n -> p (c n)"),
                                     ACT.Copy).then_inc(seq_out, 1)

            for p, chunks in enumerate(VALUE_PANELS):
                even, odd, last = (through_page(chunks, PAGES), through_page(chunks, 2 * PAGES), chunks + 2 * PAGES)
                split_hi(even - 1)
                sums_out(2 * p)
                if p == 0:
                    split_hi(2)
                    sc.wait_ge(o_sumsq, G_PAIRS)
                    nc.scalar.activation(o_sqp[:].rearrange("p h n -> p (h n)"), ps[:, 6], ACT.Sqrt,
                                         bias=eps[:, 1:2], scale=1.0 / VD).then_inc(o_std, 1)
                split_hi(odd - even - (2 if p == 0 else 0))
                sums_out(2 * p + 1)
                split_hi(last - odd)
                if chunks == K_CH:
                    take_out(p % 2, last, ACT.Sigmoid, lambda m: sig_all[:, 2 * DT - 8 + MC * p + m])
                else:
                    at_.skip_panel(p % 2, last)
                if p == 1:
                    nc.scalar.activation(warm[:], eps[:, 1:2], ACT.Sqrt)
                split_hi(1)
            sc.wait_ge(seqs_out, B // 2)
            nc.scalar.activation(o_sqs[:].rearrange("p (h b) -> p h b", b=B), o_all[:, :, T:N], ACT.Square).then_inc(o_square, 1)
            sc.wait_ge(o_sumsq, G_PAIRS + 1)
            nc.scalar.activation(o_sqs[:], ps[:, 0, 0:B * HEADS], ACT.Sqrt,
                                 bias=eps[:, 1:2], scale=1.0 / VD).then_inc(o_std, 1)
            sc.wait_ge(o_scaled, 1)
            for t in range(0, AT, KC):
                nc.scalar.activation(o_hi[:, t:t + KC], o_all[:, t:t + KC], ACT.Copy).then_inc(o_hi_ready, 1)
            panels_m = Count()
            with loop(sc, OUT_PAIRS, *at_.steps(A_CH), (panels_m, 2)) as i:
                for banks in range(2):
                    split_hi(A_CH - 1)
                    at_.skip_panel(banks, A_CH)
                    sc.wait_ge(m_sum, panels_m.add())
                    four = bass.ds(i * 8 + MC * banks, MC)
                    nc.scalar.activation(m_hi[:, four], sig[:, 1, four], ACT.Copy).then_inc(m_hi_ready, 1)
                    split_hi(1)
            out_and_norm(2, K_CH)
            ffn(norm=3)

        @block.vector
        def _(v):
            at_ = Progress()
            n, out_n = at_.split, at_.out
            own = Count()
            panels_h = Count()
            V = nc.vector

            def then(ins):
                ins.then_inc(dve_step, 1)
                v.wait_ge(dve_step, own.add())

            def split_lo(times, page=None):
                for _ in range(times):
                    s = n.n % RING
                    if page is not None and n.n % 2 == 1:
                        page()
                    v.wait_ge(w_hi_ready, n.add())
                    at_.landed[s].add(16)
                    V.tensor_tensor(w_lo[:, s], w_raw[:, s], w_hi[:, s].bitcast(F32), ALU.subtract).then_inc(w_lo_ready, 1)

            def wait_tile(m, chunks):
                if m == 0:
                    at_.chunks.add(chunks)
                if m < MC - 1:
                    v.wait_ge(tile_done, at_.tiles.add())
                else:
                    v.wait_ge(w_used, at_.chunks())

            def residual(t0, shifted=False):
                part = y[:, bass.ds(t0, MC)]
                then(V.tensor_tensor(part, x_hi[:, bass.ds(t0, MC)].bitcast(F32),
                                     x_lo[:, bass.ds(t0, MC)].bitcast(F32), ALU.add))
                if shifted:
                    then(V.tensor_tensor(part, part, over_tiles(shift[:], MC), ALU.subtract))

            def residual_panel(banks, chunks, t0, factor, after=lambda m: None):
                for m in range(MC):
                    wait_tile(m, chunks)
                    tile = y[:, bass.ds(t0 + m, 1)].rearrange("p a n -> p (a n)")
                    V.scalar_tensor_tensor(tile, ps[:, 4 * banks + m, 0:N], factor, tile,
                                           ALU.mult, ALU.add).then_inc(out_of[banks], 1)
                    out_n[banks].add()
                    after(m)

            def over_tiles(x, tiles):
                return x.rearrange("p (a n) -> p a n", a=1).broadcast_to([P, tiles, N])

            def sum_tiles(dst, src):
                return V.tensor_reduce(dst[:], src.rearrange("p t n -> p n t"), AX, ALU.add)

            def out_and_norm(k, chunks, factor):
                first, most = slice(0, 2 * MC), slice(0, 3 * MC)
                with loop(v, OUT_PAIRS - 1, *at_.steps(chunks), (own, 2)) as i:
                    for banks in range(2):
                        split_lo(chunks - 1)
                        residual(i * 8 + MC * banks)
                        residual_panel(banks, chunks, i * 8 + MC * banks, factor)
                        split_lo(1)
                for banks in range(2):
                    v.wait_ge(out_of[banks], out_n[banks]())
                sum_tiles(one_sum, y[:, first]).then_inc(ln_first, 1)
                split_lo(LEAD)
                v.wait_ge(ln_first_sum, k)
                then(V.tensor_scalar(shift[:], ps[:, 4, 0:N], 1.0 / (2 * MC * P), None, ALU.mult))
                V.tensor_tensor(y[:, first], y[:, first], over_tiles(shift[:], 2 * MC), ALU.subtract).then_inc(ln_shifted, 1)
                split_lo(chunks - 1 - LEAD)
                residual(2 * MC, shifted=True)
                residual_panel(0, chunks, 2 * MC, factor)
                v.wait_ge(out_of[0], out_n[0]())
                v.sem_inc(ln_shifted, 1)
                split_lo(1)
                sum_tiles(one_sum, y[:, most])
                split_lo(2)
                v.wait_ge(ln_squared, 6 * k - MC)
                sum_tiles(sq_sum, y_norm[:, most]).then_inc(ln_partial, 1)
                residual(3 * MC, shifted=True)
                split_lo(chunks - 3 - (LEAD - 1 if k == NORMS else 0))

                def pair_sums(m):
                    first = DT - MC + m - 1
                    if m % 2 == 1:
                        v.wait_ge(out_of[1], out_n[1]())
                        V.tensor_tensor((mean, mean_sq)[m // 2][:], y[:, first], y[:, first + 1], ALU.add).then_inc(ln_pairs, 1)
                        v.wait_ge(ln_squared, 6 * k - MC + m + 1)
                        V.tensor_tensor(y_norm[:, first], y_norm[:, first], y_norm[:, first + 1], ALU.add).then_inc(ln_pairs, 1)

                residual_panel(1, chunks, 3 * MC, factor, after=pair_sums)
                v.wait_ge(ln_sums, 2 * k - 1)
                then(V.tensor_scalar(mean[:], ps[:, 0, 0:N], 1.0 / D, None, ALU.mult))
                then(V.tensor_tensor(mean_sq[:], mean[:], mean[:], ALU.mult))
                v.wait_ge(ln_sums, 2 * k)
                V.scalar_tensor_tensor(mean_sq[:], ps[:, 1, 0:N], 1.0 / D, mean_sq[:], ALU.mult,
                                       ALU.subtract).then_inc(ln_var, 1)
                if k < NORMS:
                    split_lo(1)
                v.wait_ge(ln_std, k)
                then(V.reciprocal(rstd[:], rstd[:]))

                for i in range(DT // KC):
                    two = slice(KC * i, KC * (i + 1))
                    then(V.tensor_tensor(y[:, two], y[:, two], over_tiles(mean[:], KC), ALU.subtract))
                    V.tensor_tensor(y_norm[:, two], y[:, two], over_tiles(rstd[:], KC), ALU.mult).then_inc(ln_scaled, 1)
                    if k < NORMS and i == 1:
                        low_part(V, v, k, 0, dve_step, own)

            def ffn(norm):
                with loop(v, FFN_PAIRS, *at_.steps(K_CH), (panels_h, 1)) as i:
                    split_lo(2 * K_CH - 1)
                    at_.skip_panel(0, K_CH)
                    for m in range(MC):
                        v.wait_ge(out_of[0], out_n[0](m + 1 - MC))
                        wait_tile(m, K_CH)
                        V.tensor_tensor(hid[:, m], hid[:, m], ps[:, MC + m, 0:N], ALU.mult).then_inc(out_of[1], 1)
                    out_n[1].add(MC)
                    split_lo(1)
                    v.wait_ge(h_hi_ready, panels_h.add())
                    V.tensor_tensor(h_lo[:, bass.ds(i * MC, MC)], hid[:],
                                    h_hi[:, bass.ds(i * MC, MC)].bitcast(F32), ALU.subtract).then_inc(h_ready, 1)
                out_and_norm(norm, H_CH, 0.5 / ALPHA)

            def z_pair(page=None):
                split_lo(2 * K_CH, page)
                at_.skip_panel(0, K_CH)
                at_.skip_panel(1, K_CH)

            k_turn = Count()

            def page_scores(seq):
                def one():
                    j = k_turn.n % PAGES
                    keys = k_slots[k_turn.n % 4 if k_turn.n < 2 * PAGES else j % 2]
                    v.wait_ge(k_mult, k_turn.add())
                    dst = scores_flat[:, bass.ds(seq * (SLOTS * 16) + j * 16, 16)]
                    V.tensor_reduce(dst, keys.rearrange("p (g d) -> p g d", d=HD), AX, ALU.add).then_inc(k_free, 1)
                return one

            scores_flat = scores[:].rearrange("p b s c -> p (b s c)")

            def rope():
                for rows, j0, j1 in ((P, 0, PT), (B, PT, PT + 1)):
                    w = j1 - j0
                    x = qk_tok[0:rows, j0:j1].rearrange("p j (g d) -> p j g d", d=HD)
                    x1, x2 = x[:, :, :, 0:ROT], x[:, :, :, ROT:2 * ROT]
                    cos, sin = (rope_cs[0:rows, f, j0:j1].rearrange("p j (a r) -> p j a r", a=1)
                                .broadcast_to([rows, w, 16, ROT]) for f in range(2))
                    t = [rope_t[0:rows, k, 0:w] for k in range(4)]
                    V.tensor_tensor(t[0], x1, cos, ALU.mult)
                    V.tensor_tensor(t[1], x2, sin, ALU.mult)
                    V.tensor_tensor(t[2], x2, cos, ALU.mult)
                    then(V.tensor_tensor(t[3], x1, sin, ALU.mult))
                    V.tensor_tensor(x1, t[0], t[1], ALU.subtract)
                    ins = V.tensor_tensor(x2, t[2], t[3], ALU.add)
                    if j0 == 0:
                        then(ins)
                ins.then_inc(roped, 1)

            v.sem_inc(w_lo_ready, RING)
            v.sem_inc(k_free, 2)
            v.sem_inc(h_ready, 1)
            for i in range(QUARTERS):
                if i < LEAD:
                    split_lo(1)
                v.wait_ge(x_hi_ready, i + 1)
                q = slice(DT // QUARTERS * i, DT // QUARTERS * (i + 1))
                V.tensor_tensor(x_lo[:, q], y_norm[:, q], x_hi[:, q].bitcast(F32), ALU.subtract
                                ).then_inc(x_ready, DT // QUARTERS // KC)
            v.wait_ge(const_in, CONSTS)
            v.wait_ge(made, MADE)
            for c in range(2):
                V.tensor_tensor(lam_prod[:, c:c + 1], lam_in[:, 2 * c:2 * c + 1], lam_in[:, 2 * c + 1:2 * c + 2],
                                ALU.mult).then_inc(lam_prod_ready, 1)
            V.tensor_scalar(neg_eye[:], ident[0:B, 0:B], -NEG, NEG, ALU.mult, ALU.add)
            then(V.tensor_scalar(subln[:], subln[:], 1.0 - LAMBDA_INIT, None, ALU.mult))
            ffn(norm=1)
            z_pair()
            v.wait_ge(tok_ready, 3)
            rope()
            v.wait_ge(roped, 1)
            V.tensor_copy(q_s[:], qk_tok[0:B, PT]).then_inc(q_kept, 1)
            z_pair()
            v.wait_ge(lam_exp, 1)
            then(V.tensor_tensor(lam[:, 2:3], lam[:, 1:2], lam[:, 0:1], ALU.subtract))
            then(V.tensor_scalar(lam[:, 2:3], lam[:, 2:3], -LAMBDA_INIT, None, ALU.add))
            for x in range(LEAD, 2 * K_CH + LEAD):
                split_lo(1)
                while k_turn.n < min(x, 2 * PAGES):
                    page_scores(k_turn.n // PAGES)()
            at_.skip_panel(0, K_CH)
            at_.skip_panel(1, K_CH)
            v.wait_ge(tok_ready, 7)
            rope()
            v.wait_ge(roped, 2)
            split_lo(2, page_scores(2))
            v.wait_ge(q_stored, 16)
            then(V.tensor_tensor(q_s[:], q_s[:], qk_tok[0:B, PT], ALU.mult))
            V.memset(scores[:, :, PAGES], NEG)
            then(V.tensor_reduce(s_tmp[:, 0], q_s[:].rearrange("p (g d) -> p g d", d=HD), AX, ALU.add))
            new = scores[0:B, :, PAGES]
            then(V.tensor_tensor(new, s_tmp[:, 0:1].broadcast_to([B, B, 16]),
                                 ident[0:B, 0:B].rearrange("p (b a) -> p b a", a=1).broadcast_to([B, B, 16]), ALU.mult))
            then(V.tensor_tensor(new, new,
                                 neg_eye[:].rearrange("p (b a) -> p b a", a=1).broadcast_to([B, B, 16]), ALU.add))
            v.sem_inc(new_scored, 1)

            def prompt_max(h):
                v.wait_ge(sc_done, h + 1)
                if h >= 1:
                    v.wait_ge(at_ready, h)
                for c in range(2):
                    V.scalar_tensor_tensor(prob[:, c].rearrange("p b k -> p (b k)"), ps[:, 4 + c, 0:3 * P], SCALE,
                                           mask[:].rearrange("p b k -> p (b k)"), ALU.mult, ALU.add).then_inc(sc_masked, 1)
                v.wait_ge(sc_masked, 2 * (h + 1))
                for c in range(2):
                    V.tensor_reduce(stats[:, 2 * c:2 * c + 1], prob[:, c, 0], AX, ALU.max)
                    ins = V.tensor_reduce(stats[:, 2 * c + 1:2 * c + 2],
                                          prob[:, c, 1:3].rearrange("p b k -> p (b k)"), AX, ALU.max)
                then(ins)
                V.tensor_scalar(stats[:, 4:8], stats[:, 0:4], -1.0, None, ALU.mult).then_inc(sc_max, 1)

            def prompt_attn(h):
                v.wait_ge(sc_exp, 4 * (h + 1))
                then(V.reciprocal(stats[:, 12:16], stats[:, 8:12]))
                then(V.tensor_scalar(stats[:, 14:16], stats[:, 14:16], lam[:, 2:3], None, ALU.mult))
                if h >= 1:
                    v.wait_ge(at_turned, h)
                parts = ((0, slice(0, 1)), (1, slice(1, 3)))
                for j, b in parts:
                    ins = V.tensor_scalar(attn[:, b], prob[:, 0, b], stats[:, 12 + j:13 + j], None, ALU.mult)
                then(ins)
                for j, b in parts:
                    ins = V.scalar_tensor_tensor(attn[:, b].rearrange("p b k -> p (b k)"),
                                                 prob[:, 1, b].rearrange("p b k -> p (b k)"),
                                                 stats[:, 14 + j:15 + j],
                                                 attn[:, b].rearrange("p b k -> p (b k)"), ALU.mult, ALU.add)
                ins.then_inc(at_ready, 1)

            chunks_c = 2 * C_PAIRS * K_CH
            for x in range(LEAD + 2, chunks_c + LEAD):
                if x % 2 == 1 and k_turn.n < (2 + C_PAIRS) * PAGES:
                    page_scores(k_turn.n // PAGES)()
                split_lo(1)
                for h in range(HEADS):
                    if x == at_head(h) + RING:
                        prompt_max(h)
                    if x == at_head(h) + RING + 2:
                        prompt_attn(h)
            at_.chunks.add(chunks_c)
            at_.tiles.add(2 * C_PAIRS * (MC - 1))
            out_n[0].add(2 * C_PAIRS * MC)

            def head_norm(i, page):
                v.wait_ge(o_std, i + 1)
                for j in range(2):
                    then(V.reciprocal(o_sqp[:, j], o_sqp[:, j]))
                    o = o_all[:, bass.ds(i * 2 + j, 1), 0:T].rearrange("p a n -> p (a n)")
                    ins = V.scalar_tensor_tensor(o, o, subln[:], o_sqp[:, j], ALU.mult, ALU.mult)
                    if j == 1:
                        ins.then_inc(o_normed, 1)
                    split_lo(1, page)

            page = page_scores(2 + C_PAIRS)
            v.wait_ge(out_of[0], out_n[0]())
            then(V.tensor_tensor(u, z_c[:, 2], z_c[:, 1], ALU.mult))
            v.sem_inc(conv_new_ready, 1)
            split_lo(2, page)
            V.tensor_copy(conv_new[:, :, :, 0], conv_state[:, :, :, 1]).then_inc(conv_new_ready, 1)
            V.tensor_copy(conv_new[:, :, :, 1], u[:, :, T:N]).then_inc(conv_new_ready, 1)
            taps = [conv_state[:, :, :, 0], conv_state[:, :, :, 1], u[:, :, T:N]]
            for j in range(3):
                ins = V.tensor_tensor(conv_t[:, j], taps[j],
                                      conv_w[:, j].rearrange("p (t a) -> p t a", a=1).broadcast_to([P, AT, B]), ALU.mult)
            then(ins)
            for t in range(AT):
                ins = V.tensor_scalar(conv_o[:, t, 0:T], u[:, t, 0:T], conv_w[:, 2, t:t + 1], None, ALU.mult)
            then(ins)
            split_lo(2, page)
            for back in (1, 2):
                for t in range(AT):
                    ins = V.scalar_tensor_tensor(conv_o[:, t, back:T], u[:, t, 0:T - back], conv_w[:, 2 - back, t:t + 1],
                                                 conv_o[:, t, back:T], ALU.mult, ALU.add)
                then(ins)
                split_lo(2, page)
            then(V.tensor_tensor(conv_t[:, 0], conv_t[:, 0], conv_t[:, 1], ALU.add))
            then(V.tensor_tensor(conv_o[:, :, T:N], conv_t[:, 0], conv_t[:, 2], ALU.add))
            V.tensor_tensor(conv_o, conv_o, z_c[:, 0], ALU.mult).then_inc(conv_done, 1)
            head_norm(0, page)
            split_lo(2 * K_CH - 10, page)
            at_.skip_panel(0, K_CH)
            at_.skip_panel(1, K_CH)
            v.wait_ge(conv_hi, 1)
            v.wait_ge(conv_stored, 16 * 2)
            V.tensor_tensor(yc_lo[:], conv_o, yc_hi[:].bitcast(F32), ALU.subtract).then_inc(yc_ready, 1)

            with loop(v, G_PAIRS - 2, *at_.steps(K_CH), (k_turn, PAGES), (own, 2)) as i:
                page = page_scores(i + (3 + C_PAIRS))
                split_lo(HEAD_NORM + 2, page)
                head_norm(i + 1, page)
                split_lo(2 * K_CH - (HEAD_NORM + 2) - 2, page)
                at_.skip_panel(0, K_CH)
                at_.skip_panel(1, K_CH)

            def gate_tile(c, t):
                return sig[:, c, bass.ds(t, 1)].rearrange("p a n -> p (a n)")

            for banks in range(2):
                v.wait_ge(out_of[banks], out_n[banks]())

            def conv_gated(banks, t0, chunks):
                for m in range(MC):
                    wait_tile(m, chunks)
                    g = sig[:, 1, t0 + m]
                    V.tensor_tensor(g, g, ps[:, 4 * banks + m, 0:N], ALU.mult).then_inc(out_of[banks], 1)
                    out_n[banks].add()

            v.wait_ge(k_free, 2 + B * PAGES)
            V.tensor_reduce(s_max[:].rearrange("p (b c) -> p b c", b=B), scores[:].rearrange("p b s c -> p b c s"),
                            AX, ALU.max).then_inc(ss_max1, 1)
            v.wait_ge(ss_turned, 1)
            then(V.tensor_reduce(s_col[:], ps[:, 7, 0:P], AX, ALU.max))
            V.tensor_scalar(s_diag[:], ident[:], s_col[:], None, ALU.mult).then_inc(ss_diag, 1)
            split_lo(A_CH)
            v.wait_ge(ss_bcast, 1)
            top_score = ps[:, 7, 0:P].rearrange("p (b a c) -> p b a c", b=B, a=1).broadcast_to([P, B, SLOTS, 16])
            V.tensor_tensor(scores[:], scores[:], top_score, ALU.subtract).then_inc(ss_shift, 1)
            conv_gated(0, 0, A_CH)
            split_lo(1)
            v.wait_ge(ss_exp, 1)
            V.tensor_reduce(s_max[:].rearrange("p (b c) -> p b c", b=B), scores[:].rearrange("p b s c -> p b c s"),
                            AX, ALU.add).then_inc(ss_sums, 1)
            split_lo(1)
            v.wait_ge(ss_den, 1)
            then(V.reciprocal(s_rec[:], ps[:, 0, 0:P]))
            v.sem_inc(ss_rec, 1)
            rec = s_rec[:].rearrange("p (b a h c) -> p b a h c", b=B, a=1, c=2)
            then(V.tensor_scalar(rec[:, :, 0, :, 1], rec[:, :, 0, :, 1], lam[:, 2:3], None, ALU.mult))
            e = scores[:].rearrange("p b s (h c) -> p b s h c", c=2)
            V.tensor_tensor(s_attn[:], e[:, :, :, :, 0], rec[:, :, :, :, 0].broadcast_to([P, B, SLOTS, HEADS]), ALU.mult)
            then(V.tensor_tensor(s_attn2[:], e[:, :, :, :, 1], rec[:, :, :, :, 1].broadcast_to([P, B, SLOTS, HEADS]), ALU.mult))
            V.tensor_tensor(own_head[:], ident[0:2 * HEADS, 0:HEADS], ident[0:2 * HEADS, HEADS:2 * HEADS], ALU.add)
            V.tensor_tensor(s_attn[:], s_attn[:], s_attn2[:], ALU.add).then_inc(ss_attn, 1)
            split_lo(2)
            v.wait_ge(pv_weights_hi, 1)
            V.tensor_tensor(s_weights[:, :, :, 1], s_attn[:, :, 0:PAGES], s_weights[:, :, :, 0].bitcast(F32),
                            ALU.subtract).then_inc(pv_weights, 1)
            conv_gated(1, MC, A_CH)

            def seqs_result(p):
                v.wait_ge(seq_turned, 2 * (p + 1))
                b = 2 * p
                V.tensor_copy(o_all[:, :, T + b:T + b + 2].rearrange("p h b -> p b h"),
                              ps[:, 7 - 4 * (p % 2), b * HEADS:(b + 2) * HEADS].rearrange("p (b h) -> p b h", b=2)
                              ).then_inc(seqs_out, 1)

            for p, chunks in enumerate(VALUE_PANELS):
                last = chunks + 2 * PAGES
                if p == 0:
                    split_lo(through_page(K_CH, PAGES) + 1)
                    head_norm(G_PAIRS - 1, None)
                    split_lo(last - 1 - through_page(K_CH, PAGES) - 1 - 2)
                else:
                    split_lo(last - 1)
                if chunks == K_CH:
                    at_.skip_panel(p % 2, last)
                else:
                    conv_gated(p % 2, p * MC, last)
                seqs_result(p)
                split_lo(1)
            v.wait_ge(o_std, G_PAIRS + 1)
            then(V.reciprocal(o_sqs[:], o_sqs[:]))
            then(V.scalar_tensor_tensor(o_all[:, :, T:N], o_all[:, :, T:N], subln[:],
                                        o_sqs[:].rearrange("p (h b) -> p h b", b=B), ALU.mult, ALU.mult))
            v.sem_inc(o_scaled, 1)
            for t in range(0, AT, KC):
                v.wait_ge(o_hi_ready, t // KC + 1)
                V.tensor_tensor(o_lo[:, t:t + KC], o_all[:, t:t + KC], o_hi[:, t:t + KC].bitcast(F32),
                                ALU.subtract).then_inc(o_split, 1)
            panels_m = Count()
            with loop(v, OUT_PAIRS, *at_.steps(A_CH), (panels_m, 2)) as i:
                for banks in range(2):
                    split_lo(A_CH - 1)
                    for m in range(MC):
                        wait_tile(m, A_CH)
                        g = gate_tile(0, i * 8 + (MC * banks + m))
                        V.tensor_tensor(g, g, ps[:, 4 * banks + m, 0:N], ALU.mult).then_inc(out_of[banks], 1)
                        out_n[banks].add()
                    v.wait_ge(out_of[banks], out_n[banks]())
                    four = bass.ds(i * 8 + MC * banks, MC)
                    V.tensor_tensor(sig[:, 1, four], sig[:, 1, four], sig[:, 0, four], ALU.add).then_inc(m_sum, 1)
                    split_lo(1)
                    v.wait_ge(m_hi_ready, panels_m.add())
                    V.tensor_tensor(m_lo[:, four], sig[:, 1, four], m_hi[:, four].bitcast(F32), ALU.subtract).then_inc(m_ready, 1)
            out_and_norm(2, K_CH, 1.0 / ALPHA)
            ffn(norm=3)


def rope_tables():
    inv = np.power(np.float32(500000.0), -np.arange(0, 2 * ROT, 2, dtype=np.float32) / np.float32(2 * ROT))
    pos = np.full((P, 3), PAGE * PAGES, np.float32)
    for j in range(PT):
        pos[:, j] = np.arange(j * P, (j + 1) * P)
    ang = (pos[:, :, None] * inv.astype(np.float32)).astype(np.float32)
    return np.stack([np.cos(ang), np.sin(ang)], axis=1).astype(np.float32)


_PLAIN = ["cache_k", "cache_v", "ffn1_w_gate", "ffn1_w_up", "ffn1_w_down", "w_in", "w_attn_out", "w_conv_out",
          "w_o", "ffn2_w_gate", "ffn2_w_up", "ffn2_w_down"]
_OUTS = {"y_t": (D, N), "k_prompt": (T, DC), "v_prompt": (T, DC), "k_sample": (B, DC), "v_sample": (B, DC),
         "conv_prompt_t": (DC, 2), "conv_sample_t": (DC, B, 2)}


def kernel(**inputs):
    import concourse.bacc as bacc
    from concourse.bass_utils import run_bass_kernel_spmd

    x = {k: np.asarray(v) for k, v in inputs.items()}
    feats = lambda v, t: v.reshape(-1, t, P).transpose(2, 0, 1)
    arrays = {k: x[k] for k in _PLAIN}
    arrays |= {
        "x_prompt_t": x["x_prompt"][0].T,
        "x_sample_t": x["x_sample"][:, 0].T,
        "page_table": x["page_table"].reshape(1, -1),
        "ln_g": feats(x["ln_g"], DT), "ln_b": feats(x["ln_b"], DT), "conv_w": feats(x["conv_w"], AT),
        "state_conv": x["state_conv"][0].reshape(B, 2, AT, P).transpose(3, 2, 0, 1),
        "rope": rope_tables(),
        "subln_g": x["subln_g"].reshape(P, 1),
        "lambdas": np.concatenate([x["lambda_" + k] for k in ("q1", "k1", "q2", "k2")]).T,
    }
    nc = bacc.Bacc("TRN2", target_bir_lowering=False, num_devices=1)
    feed, args, outs = {}, {}, {}
    for name, v in arrays.items():
        v = np.ascontiguousarray(v)
        feed["in_" + name] = v
        args[name] = nc.dram_tensor("in_" + name, v.shape, mybir.dt.from_np(v.dtype), kind="ExternalInput").ap()
    for name, shape in _OUTS.items():
        outs[name] = nc.dram_tensor("out_" + name, shape, F32, kind="ExternalOutput").ap()
    program(nc, args, outs)
    r = run_bass_kernel_spmd(nc, [feed], core_ids=[0]).results[0]
    r = {k: r["out_" + k] for k in _OUTS}
    yt = r["y_t"].T
    heads = (HEADS, VD)
    return (yt[:T].reshape(1, T, D), yt[T:].reshape(B, 1, D),
            r["k_prompt"].reshape(1, 1, T, *heads), r["v_prompt"].reshape(1, 1, T, *heads),
            r["conv_prompt_t"].T.reshape(1, 1, 2, DC),
            r["k_sample"].reshape(1, B, 1, *heads), r["v_sample"].reshape(1, B, 1, *heads),
            r["conv_sample_t"].transpose(1, 2, 0).reshape(1, B, 2, DC))
```
